# Optimizing a Trainium2 kernel written in Bass

```python
import jax, jax.numpy as jnp
from jax import lax
import numpy as np

D_MODEL = 1024
BATCH = 1
SEQ = 512
DEPTH = 1

PLE_DIM = 256
SB_HEADS = 8
SB_HEAD_DIM = 64
SB_BLOCK = 128
RET_HEADS = 8
RET_QK_DIM = 64
RET_V_DIM = 128
RET_CHUNK = 128
ROPE_BASE = 10000.0
D_FF = 2816
CONV_WIDTH = 3
EPS = 1e-6

SB_W = SB_HEADS * SB_HEAD_DIM
RET_QK_W = RET_HEADS * RET_QK_DIM
RET_V_W = RET_HEADS * RET_V_DIM
IN_SPLITS = (SB_W, SB_W, SB_W, RET_QK_W, RET_QK_W, RET_V_W, RET_V_W, D_MODEL, D_MODEL)
D_IN = SB_W * 3 + RET_QK_W * 2 + RET_V_W * 2 + D_MODEL * 2

kernel_name = "hybrid_stickbreak_retention_convglu_ple"

def rmsnorm(x, gain):
    xf = x.astype(jnp.float32)
    xf = xf * lax.rsqrt(jnp.mean(xf * xf, axis=-1, keepdims=True) + EPS)
    return (xf * gain.astype(jnp.float32)).astype(x.dtype)

def head_rmsnorm(x, gain):
    xf = x.astype(jnp.float32)
    xf = xf * lax.rsqrt(jnp.mean(xf * xf, axis=-1, keepdims=True) + EPS)
    return (xf * gain.astype(jnp.float32)[None, :, None, :]).astype(x.dtype)

def split_cols(y):
    out = []
    off = 0
    for w in IN_SPLITS:
        out.append(y[..., off:off + w])
        off += w
    return out

def to_heads(t, n_heads):
    b, s, _ = t.shape
    return t.reshape(b, s, n_heads, -1).transpose(0, 2, 1, 3)

def from_heads(t):
    b, h, s, d = t.shape
    return t.transpose(0, 2, 1, 3).reshape(b, s, h * d)

def rotary(x):
    s, d = x.shape[2], x.shape[3]
    half = d // 2
    inv = ROPE_BASE ** (-jnp.arange(half, dtype=jnp.float32) * 2.0 / d)
    ang = jnp.arange(s, dtype=jnp.float32)[:, None] * inv[None, :]
    cos, sin = jnp.cos(ang), jnp.sin(ang)
    xf = x.astype(jnp.float32)
    x1, x2 = xf[..., :half], xf[..., half:]
    return jnp.concatenate([x1 * cos - x2 * sin, x1 * sin + x2 * cos], axis=-1).astype(x.dtype)

def stick_breaking_attention(q, k, v):
    s_len, d = q.shape[2], q.shape[3]
    scale = d ** -0.5
    outs = []
    for i in range(s_len // SB_BLOCK):
        t0 = i * SB_BLOCK
        n_keys = t0 + SB_BLOCK
        qb = q[:, :, t0:t0 + SB_BLOCK]
        kk = k[:, :, :n_keys]
        vv = v[:, :, :n_keys]
        z = jnp.einsum('bhtd,bhsd->bhts', qb, kk).astype(jnp.float32) * scale
        qpos = t0 + jnp.arange(SB_BLOCK)[:, None]
        kpos = jnp.arange(n_keys)[None, :]
        causal = kpos < qpos
        log_one_minus = jnp.where(causal, -jax.nn.softplus(z), 0.0)
        suffix = lax.cumsum(log_one_minus, axis=3, reverse=True) - log_one_minus
        log_a = jax.nn.log_sigmoid(z) + suffix
        a = jnp.where(causal, jnp.exp(log_a), 0.0).astype(v.dtype)
        outs.append(jnp.einsum('bhts,bhsd->bhtd', a, vv))
    return jnp.concatenate(outs, axis=2)

def retention_chunkwise(q, k, v):
    b, h, s_len, dk = q.shape
    dv = v.shape[3]
    c = RET_CHUNK
    n_chunks = s_len // c
    log_gamma = jnp.log1p(-jnp.exp2(-5.0 - jnp.arange(h, dtype=jnp.float32)))
    idx = jnp.arange(c, dtype=jnp.float32)
    diff = idx[:, None] - idx[None, :]
    d_local = jnp.where(diff >= 0.0,
                        jnp.exp(jnp.maximum(diff, 0.0)[None] * log_gamma[:, None, None]), 0.0)
    xi = jnp.exp((idx + 1.0)[None, :] * log_gamma[:, None])
    zeta = jnp.exp((c - 1.0 - idx)[None, :] * log_gamma[:, None])
    g_chunk = jnp.exp(c * log_gamma)

    def chunked(t):
        return jnp.moveaxis(t.reshape(b, h, n_chunks, c, t.shape[3]), 2, 0)

    def step(state, inp):
        qc, kc, vc = inp
        inner = jnp.einsum('bhid,bhjd->bhij', qc, kc) * d_local[None]
        y = (jnp.einsum('bhij,bhje->bhie', inner, vc)
             + jnp.einsum('bhid,bhde->bhie', qc, state) * xi[None, :, :, None])
        new_state = (state * g_chunk[None, :, None, None]
                     + jnp.einsum('bhjd,bhje->bhde', kc * zeta[None, :, :, None], vc))
        return new_state, y

    state0 = jnp.zeros((b, h, dk, dv), jnp.float32)
    _, ys = lax.scan(step, state0, (chunked(q), chunked(k), chunked(v)))
    return jnp.moveaxis(ys, 0, 2).reshape(b, h, s_len, dv).astype(v.dtype)

def causal_depthwise_conv(a, w, bias):
    s_len = a.shape[1]
    padded = jnp.pad(a, ((0, 0), (CONV_WIDTH - 1, 0), (0, 0)))
    out = bias
    for j in range(CONV_WIDTH):
        out = out + w[j] * padded[:, j:j + s_len]
    return out

def hybrid_layer(x, p_i, g_mix, w_in, sb_q_gain, sb_k_gain, ret_norm_gain,
                 w_branch_sb, w_branch_ret, w_out, g_ffn, w_up, conv_w, conv_b,
                 w_down, g_ple, w_ple_gate, w_ple_proj):
    h = rmsnorm(x, g_mix)
    q_sb, k_sb, v_sb, q_r, k_r, v_r, g_r, gate_sb, gate_ret = split_cols(h @ w_in)

    q_sb = head_rmsnorm(to_heads(q_sb, SB_HEADS), sb_q_gain)
    k_sb = head_rmsnorm(to_heads(k_sb, SB_HEADS), sb_k_gain)
    y_sb = from_heads(stick_breaking_attention(q_sb, k_sb, to_heads(v_sb, SB_HEADS)))

    q_r = rotary(to_heads(q_r, RET_HEADS))
    k_r = rotary(to_heads(k_r, RET_HEADS)) * (RET_QK_DIM ** -0.5)
    y_r = retention_chunkwise(q_r, k_r, to_heads(v_r, RET_HEADS))
    y_r = from_heads(head_rmsnorm(y_r, ret_norm_gain)) * jax.nn.silu(g_r)

    merged = (jax.nn.sigmoid(gate_sb) * (y_sb @ w_branch_sb)
              + jax.nn.sigmoid(gate_ret) * (y_r @ w_branch_ret))
    x = x + merged @ w_out

    h = rmsnorm(x, g_ffn)
    up = h @ w_up
    a, u = up[..., :D_FF], up[..., D_FF:]
    a = causal_depthwise_conv(a, conv_w, conv_b)
    x = x + (jax.nn.gelu(a) * u) @ w_down

    gate = jax.nn.sigmoid(rmsnorm(x, g_ple) @ w_ple_gate)
    x = x + gate * (p_i @ w_ple_proj)
    return x

def setup_inputs(seed: int = 0) -> dict:
    key = jax.random.key(seed)
    ks = jax.random.split(key, 20)

    def nrm(k, shape, fan_in):
        return jax.random.normal(k, shape, jnp.float32) * (fan_in ** -0.5)

    def gain(k, shape):
        return 1.0 + 0.1 * jax.random.normal(k, shape, jnp.float32)

    L = DEPTH
    return {
        "x": jax.random.normal(ks[0], (BATCH, SEQ, D_MODEL), jnp.float32),
        "p": jax.random.normal(ks[1], (DEPTH, BATCH, SEQ, PLE_DIM), jnp.float32),
        "g_mix": gain(ks[2], (L, D_MODEL)),
        "w_in": nrm(ks[3], (L, D_MODEL, D_IN), D_MODEL),
        "sb_q_gain": gain(ks[4], (L, SB_HEADS, SB_HEAD_DIM)),
        "sb_k_gain": gain(ks[5], (L, SB_HEADS, SB_HEAD_DIM)),
        "ret_norm_gain": gain(ks[6], (L, RET_HEADS, RET_V_DIM)),
        "w_branch_sb": nrm(ks[7], (L, SB_W, D_MODEL), SB_W),
        "w_branch_ret": nrm(ks[8], (L, RET_V_W, D_MODEL), RET_V_W),
        "w_out": nrm(ks[9], (L, D_MODEL, D_MODEL), D_MODEL),
        "g_ffn": gain(ks[10], (L, D_MODEL)),
        "w_up": nrm(ks[11], (L, D_MODEL, 2 * D_FF), D_MODEL),
        "conv_w": nrm(ks[12], (L, CONV_WIDTH, D_FF), CONV_WIDTH),
        "conv_b": 0.02 * jax.random.normal(ks[13], (L, D_FF), jnp.float32),
        "w_down": nrm(ks[14], (L, D_FF, D_MODEL), D_FF),
        "g_ple": gain(ks[15], (L, D_MODEL)),
        "w_ple_gate": nrm(ks[16], (L, D_MODEL, D_MODEL), D_MODEL),
        "w_ple_proj": nrm(ks[17], (L, PLE_DIM, D_MODEL), PLE_DIM),
    }

def reference(x, p, g_mix, w_in, sb_q_gain, sb_k_gain, ret_norm_gain, w_branch_sb,
              w_branch_ret, w_out, g_ffn, w_up, conv_w, conv_b, w_down, g_ple,
              w_ple_gate, w_ple_proj):
    for i in range(DEPTH):
        x = hybrid_layer(x, p[i], g_mix[i], w_in[i], sb_q_gain[i], sb_k_gain[i],
                         ret_norm_gain[i], w_branch_sb[i], w_branch_ret[i], w_out[i],
                         g_ffn[i], w_up[i], conv_w[i], conv_b[i], w_down[i], g_ple[i],
                         w_ple_gate[i], w_ple_proj[i])
    return x


_drawn_inputs = setup_inputs


def setup_inputs(seed=0):
    import zlib

    import numpy as np

    out = dict(_drawn_inputs(seed))
    spreads = {}
    factors = {'sb_q_gain': 3.773, 'sb_k_gain': 3.613, 'conv_b': 6.035, 'g_ple': 3.797}
    for name, (base, spread) in spreads.items():
        noise = np.random.default_rng([zlib.crc32(name.encode()), seed]).standard_normal(out[name].shape)
        drawn = base * np.exp(spread * noise) if base else spread * noise
        out[name] = __import__('jax').numpy.asarray(drawn.astype(out[name].dtype))
    for name, factor in factors.items():
        out[name] = (out[name] * factor).astype(out[name].dtype)
    return out
```

```python
from contextlib import ExitStack

import concourse.bass as bass
from concourse import mybir

F32 = mybir.dt.float32
F32R = mybir.dt.float32r
I32 = mybir.dt.int32
ALU = mybir.AluOpType
ACT = mybir.ActivationFunctionType

P = 128
SEQ = 512
D = 1024
KD = D // P
NT = SEQ // P
PAIRS = 4
FB = 2816 // P
PB = 256 // P
EPS = 1e-6
RING = 3

SLOTS = 9
RAW_OF = {0: 0, 1: 1, 2: 2, 3: 3, 4: 4, 7: 5, 8: 6}
RAWS = 7

GATE0 = PAIRS * SLOTS
MERGE0 = GATE0 + 6
OUT0 = MERGE0 + 4 * 6 + 2
UP0 = OUT0 + KD
DOWN0 = UP0 + 2 * FB
DOWN_K = (8, 8, 6)
PLE0 = DOWN0 + 3 * KD
PLET0 = DOWN0 + KD

T_H, T_YR, T_YS = 0, 8, 16
T_SBQ, T_SBK, T_SBV = 20, 21, 22
T_RQ, T_RK, T_RV = 23, 24, 25
T_SP, T_A = 27, 30
T_M = 20
T_G = 8
T_P = 30
N_TILES = 32

A_X = 0
A_RAW, A_SQ, A_SQY, A_SWAP, A_Y = 0, 2, (7, 3), 4, 5
A_DEC, A_COS, A_SIN, A_G, A_T, A_A = 8, 10, 11, 12, 14, 16
A_SG = (10, 14, 8)
A_RS, A_ACC, A_CONV, A_C, A_SQR, A_U = 8, 9, 10, 12, 13, 16
A_P = 14
N_F32 = 18

C_ONES, C_BLOCK, C_IDENT, C_NEGU, C_NEG1, C_MASK = range(6)
N_CONST = 6
G_MIX, G_FFN, G_PLE, G_RET, G_SBQ, G_SBK = 0, 8, 16, 24, 32, 36
N_GAIN = 40


def build(nc, xT, pT, w_in, w_a, w_b, w_out, w_up, w_down, w_pg, w_pp, g_mix, g_ffn, g_ple, g_ret, g_sbq, g_sbk,
          conv_w, conv_b, consts, decay, rope, outT):
    with ExitStack() as ctx:
        def sb(name, shape, dt):
            return ctx.enter_context(nc.sbuf_tensor(name, shape, dt))

        def sem(name):
            return ctx.enter_context(nc.semaphore(name))

        hi = sb("hi", [P, N_TILES, SEQ], F32R)
        lo = sb("lo", [P, N_TILES, SEQ], F32R)
        fs = sb("fs", [P, N_F32, SEQ], F32)
        fs_flat = fs[:, :, :].rearrange("p t n -> p (t n)")
        w_f = [sb(f"w_f{r}", [P, 8, P], F32) for r in range(RING)]
        w_hi = [sb(f"w_hi{r}", [P, 8, P], F32R) for r in range(RING)]
        w_lo = [sb(f"w_lo{r}", [P, 8, P], F32R) for r in range(RING)]
        cst = sb("cst", [P, N_CONST, P], F32)
        cr = sb("cr", [P, N_CONST, P], F32R)
        gain = sb("gain", [P, N_GAIN, 1], F32)
        cw = sb("cw", [P, 4, FB, 1], F32)
        eps = sb("eps", [P, 1], F32)

        bank = [ctx.enter_context(nc.psum_tensor(f"dense{b}", [P, SEQ], F32)) for b in range(3)]
        zbank = [ctx.enter_context(nc.psum_tensor(f"z{b}", [P, SEQ], F32)) for b in range(3)]
        ybank = ctx.enter_context(nc.psum_tensor("ybank", [P, SEQ], F32))
        misc = ctx.enter_context(nc.psum_tensor("misc", [P, SEQ], F32))

        s_wdma = [sem(f"s_wdma{r}") for r in range(RING)]
        s_whi, s_wlo, s_used = sem("s_whi"), sem("s_wlo"), sem("s_used")
        s_cst, s_gain, s_eps, s_cr = sem("s_cst"), sem("s_gain"), sem("s_eps"), sem("s_cr")
        s_x = [sem(f"s_x{i}") for i in range(4)]
        s_xsq, s_xst, s_rope, s_dec = sem("s_xsq"), sem("s_xst"), sem("s_rope"), sem("s_dec")
        s_xln, s_xrs, s_hf, s_hhi, s_h = sem("s_xln"), sem("s_xrs"), sem("s_hf"), sem("s_hhi"), sem("s_h")
        s_evac = sem("s_evac")
        s_raw_done = sem("s_raw_done")
        s_sq, s_stat, s_ln, s_rs, s_nrm, s_nhi = (sem("s_sq"), sem("s_stat"), sem("s_ln"), sem("s_rs"), sem("s_nrm"),
                                                  sem("s_nhi"))
        s_vt, s_vhi = sem("s_vt"), sem("s_vhi")
        s_swap, s_rmul, s_rot, s_rhi = sem("s_swap"), sem("s_rmul"), sem("s_rot"), sem("s_rhi")
        s_misc = sem("s_misc")
        s_z, s_abs, s_e, s_l, s_sp, s_sphi, s_splo = (sem("s_z"), sem("s_abs"), sem("s_e"), sem("s_l"), sem("s_sp"),
                                                      sem("s_sphi"), sem("s_splo"))
        s_u, s_zx, s_ysum, s_yshi, s_yslo = sem("s_u"), sem("s_zx"), sem("s_ysum"), sem("s_yshi"), sem("s_yslo")
        s_ahi, s_alo = sem("s_ahi"), sem("s_alo")
        s_zr, s_zd, s_yr = sem("s_zr"), sem("s_zd"), sem("s_yr")
        s_yraw, s_ysq, s_ystat, s_yln, s_yrs = (sem("s_yraw"), sem("s_ysq"), sem("s_ystat"), sem("s_yln"),
                                                sem("s_yrs"))
        s_silu, s_yn, s_yf, s_yrhi, s_yrlo = sem("s_silu"), sem("s_yn"), sem("s_yf"), sem("s_yrhi"), sem("s_yrlo")
        s_gate, s_sig, s_madd, s_mhi, s_mlo = sem("s_gate"), sem("s_sig"), sem("s_madd"), sem("s_mhi"), sem("s_mlo")
        s_read = sem("s_read")
        s_xt, s_rsq, s_rehi, s_relo, s_acc = sem("s_xt"), sem("s_rsq"), sem("s_rehi"), sem("s_relo"), sem("s_acc")
        s_rst, s_rln, s_rrs = sem("s_rst"), sem("s_rln"), sem("s_rrs")
        s_halo, s_c0, s_c1, s_c2, s_gelu = sem("s_halo"), sem("s_c0"), sem("s_c1"), sem("s_c2"), sem("s_gelu")
        s_g, s_ghi, s_glo = sem("s_g"), sem("s_ghi"), sem("s_glo")
        s_cw, s_p, s_phi, s_plo = sem("s_cw"), sem("s_p"), sem("s_phi"), sem("s_plo")
        s_pg, s_y, s_out = sem("s_pg"), sem("s_y"), sem("s_out")

        def width(i):
            return SEQ - P * i

        def read(tile):
            return tile - (OUT0 - 17)

        def sb_unit(n):
            return n // NT, NT - 1 - n % NT

        def r_unit(n):
            return n // NT, n % NT

        def sp_cols(hd, i):
            at = 1280 if (hd == 1 and i == 3) else (0, 512, 896, 1152)[i]
            return at, at + width(i)

        def sp_view(t, hd, i):
            a, b = sp_cols(hd, i)
            return t[:, T_SP:T_SP + 3, :].rearrange("p t n -> p (t n)")[:, a:b]

        block = ctx.enter_context(nc.Block())

        @block.sync
        def _(sp):
            def load(c, r, src, kt, first=False):
                if not first:
                    sp.wait_ge(s_wlo, c - 2)
                sp.dma_start(w_f[r][:, 0:kt, :], src).then_inc(s_wdma[r], 16)

            for i in range(4):
                sp.dma_start(fs[:, A_X + 2 * i:A_X + 2 * i + 2, :], xT[:, 2 * i:2 * i + 2, :]).then_inc(s_x[i], 16)
                if i < 3:
                    load(i, i, w_in[i], 8, first=True)
            sp.dma_start(fs[:, A_COS:A_COS + 2, :], rope[:, :, :]).then_inc(s_rope, 16)
            for c in range(3, 8):
                load(c, c % RING, w_in[c], 8)

            def swap_halves(j, t):
                sp.wait_ge(s_evac, SLOTS * j + 4 + t)
                if t == 1:
                    sp.wait_ge(s_rot, 2 * j + 1)
                raw = A_RAW + (3 + t) % 2
                for b in range(4):
                    sp.dma_start(fs[32 * b:32 * b + 32, A_SWAP, :],
                                 fs[32 * (b ^ 1):32 * (b ^ 1) + 32, raw, :]).then_inc(s_swap, 16)

            def pair_loads(j, s):
                c = SLOTS * j + s + 5
                load(c, (s + 5) % RING, w_in[c], 8)
                if s == 4:
                    swap_halves(j, 0)
                    sp.dma_start(fs[:, A_DEC:A_DEC + 2, :], decay[j]).then_inc(s_dec, 16)
                if s == 5:
                    swap_halves(j, 1)

            with sp.Fori(0, PAIRS - 1) as j:
                for s in range(3, 3 + SLOTS):
                    pair_loads(j, s)
            for s in range(3, 7):
                pair_loads(PAIRS - 1, s)
            load(GATE0 + 3, 0, w_in[GATE0 + 3], 8)
            load(GATE0 + 4, 1, w_a[0], 4)
            load(GATE0 + 5, 2, w_b[0], 8)
            with sp.Fori(0, 2) as it:
                for mm in range(3):
                    c = MERGE0 + 12 * it + 4 * mm
                    m = 3 * it + (mm + 1)
                    load(c, (4 * mm) % RING, w_in[GATE0 + 2 + 2 * m], 8)
                    load(c + 1, (4 * mm + 1) % RING, w_in[GATE0 + 3 + 2 * m], 8)
                    load(c + 2, (4 * mm + 2) % RING, w_a[m], 4)
                    load(c + 3, (4 * mm + 3) % RING, w_b[m], 8)
            load(OUT0 - 2, 0, w_a[7], 4)
            load(OUT0 - 1, 1, w_b[7], 8)
            load(OUT0, OUT0 % RING, w_out[0], 8)
            with sp.Fori(0, 2) as it:
                for mm in range(3):
                    m = 3 * it + (mm + 1)
                    load(OUT0 + m, (OUT0 + 1 + mm) % RING, w_out[m], 8)
            load(OUT0 + 7, (OUT0 + 7) % RING, w_out[7], 8)
            load(UP0, UP0 % RING, w_up[0], 8)
            load(UP0 + 1, (UP0 + 1) % RING, w_up[1], 8)
            with sp.Fori(0, 7) as it:
                for q in range(6):
                    u = 6 * it + (2 + q)
                    load(UP0 + u, (UP0 + 2 + q) % RING, w_up[u], 8)
            with sp.Fori(0, KD) as m:
                for t in range(3):
                    k0 = sum(DOWN_K[:t])
                    load(DOWN0 + 3 * m + t, t, w_down[m, :, k0:k0 + DOWN_K[t], :], DOWN_K[t])

            def load_ple(m):
                load(PLE0 + 2 * m, (2 * m) % RING, w_pg[m], 8)
                load(PLE0 + 2 * m + 1, (2 * m + 1) % RING, w_pp[m], PB)

            def store(m):
                sp.wait_ge(s_y, m + 1)
                sp.dma_start(outT[m], fs[:, A_X + m, :]).then_inc(s_out, 16)

            for m in range(KD):
                load_ple(m)
                if m >= 4:
                    store(m - 4)
            for m in range(4, KD):
                store(m)
            sp.wait_ge(s_out, 16 * KD)

        @block.tensor
        def _(pe):
            mm = nc.tensor.matmul

            def split3(out, w1, w0, x1, x0, start, stop, skip=False):
                mm(out, w1, x1, start=start, stop=False, skip_group_check=skip)
                mm(out, w1, x0, start=False, stop=False, skip_group_check=skip)
                return mm(out, w0, x1, start=False, stop=stop, skip_group_check=skip)

            def chunk(c, r, b, kt, tile0, hooks=None, k_first=0, last=True, before=None):
                pe.wait_ge(s_wlo, c + 1)
                for k in range(kt):
                    if before and k in before:
                        pe.wait_ge(*before[k])
                    ins = split3(bank[b][:, :], w_hi[r][:, k, :], w_lo[r][:, k, :], hi[:, tile0 + k, :],
                                 lo[:, tile0 + k, :], start=(k_first + k == 0), stop=(last and k == kt - 1))
                    if k == kt - 1:
                        ins.then_inc(s_used, 1)
                    if hooks and k in hooks:
                        hooks[k]()

            pe.wait_ge(s_cst, 16)
            for k in range(KD):
                pe.wait_ge(s_xsq, k + 1)
                ins = mm(misc[:, :], cst[:, C_ONES, :], fs[:, A_T + k % 4, :], start=(k == 0), stop=(k == KD - 1))
                ins.then_inc(s_xst, 1)

            def stat(w, src, done):
                return mm(misc[:, :], cst[:, w, :], fs[:, src, :], start=True, stop=True).then_inc(done, 1)

            def stat_qk(j, t, free):
                pe.wait_ge(s_sq, 2 * j + t + 1)
                if free is not None:
                    pe.wait_ge(*free)
                stat(C_BLOCK, A_SQ, s_stat)

            def stat_y(j, hd, free):
                pe.wait_ge(s_ysq, 2 * j + hd + 1)
                pe.wait_ge(*free)
                stat(C_ONES, A_SQY[hd], s_ystat)

            def turn_v(j, s, free):
                pe.wait_ge(s_evac, SLOTS * j + s + 1)
                pe.wait_ge(*free)
                for i in range(NT):
                    ins = nc.tensor.transpose(misc[:, i * P:(i + 1) * P],
                                              fs[:, A_RAW + RAW_OF[s] % 2, i * P:(i + 1) * P],
                                              cst[:, C_IDENT, :])
                ins.then_inc(s_vt, 1)

            def sb_step(j, n):
                if n < 8:
                    hd, i = sb_unit(n)
                    N = width(i)
                    if n == 0:
                        pe.wait_ge(s_raw_done, RAWS * j + 2)
                    if n >= 3:
                        pe.wait_ge(s_zx, 8 * j + n - 2)
                    rows = slice(64 * hd, 64 * hd + 64)
                    z = zbank[n % 3][:, 0:N]
                    keys, qs = slice(i * P, (i + 1) * P), slice(i * P, SEQ)
                    split3(z, hi[rows, T_SBK, keys], lo[rows, T_SBK, keys], hi[rows, T_SBQ, qs], lo[rows, T_SBQ, qs],
                           start=True, stop=False, skip=True)
                    mm(zbank[n % 3][:, 0:P], cr[:, C_IDENT, :], cr[:, C_MASK, :], start=False, stop=True,
                       skip_group_check=True).then_inc(s_z, 1)
                if 2 <= n < 10:
                    u = n - 2
                    hd, i = sb_unit(u)
                    N = width(i)
                    pe.wait_ge(s_splo, 8 * j + u + 1)
                    for ii in range(i, NT):
                        w = cr[:, C_NEGU if ii == i else C_NEG1, :]
                        for part in (hi, lo):
                            ins = mm(zbank[u % 3][:, (ii - i) * P:N], w, sp_view(part, hd, ii), start=False,
                                     stop=(ii == NT - 1 and part is lo), skip_group_check=True)
                    ins.then_inc(s_u, 1)
                if n >= 3:
                    v = n - 3
                    hd, i = sb_unit(v)
                    if v == 0:
                        pe.wait_ge(s_raw_done, RAWS * j + 3)
                    if v == 4:
                        pe.wait_ge(s_yslo, 2 * j + 1)
                    pe.wait_ge(s_alo, 16 * j + v + 1)
                    cols = slice(i * P, (i + 1) * P)
                    ins = split3(ybank[:, i * P:SEQ], hi[:, T_SBV, cols], lo[:, T_SBV, cols],
                                 hi[:, T_A + v % 2, 0:width(i)], lo[:, T_A + v % 2, 0:width(i)],
                                 start=(v % NT == 0), stop=(v % NT == 3), skip=True)
                    if v % NT == 3:
                        ins.then_inc(s_ysum, 1)

            def r_step(j, n):
                if n < 8:
                    hd, i = r_unit(n)
                    if n == 0:
                        pe.wait_ge(s_raw_done, RAWS * j + 5)
                    if n >= 3:
                        pe.wait_ge(s_zd, 8 * j + n - 2)
                    rows = slice(64 * hd, 64 * hd + 64)
                    keys, qs = slice(i * P, (i + 1) * P), slice(i * P, SEQ)
                    split3(zbank[n % 3][:, 0:width(i)], hi[rows, T_RK, keys], lo[rows, T_RK, keys], hi[rows, T_RQ, qs],
                           lo[rows, T_RQ, qs], start=True, stop=True).then_inc(s_zr, 1)
                if n >= 1:
                    v = n - 1
                    hd, i = r_unit(v)
                    if v == 0:
                        pe.wait_ge(s_yslo, 2 * j + 2)
                        pe.wait_ge(s_raw_done, RAWS * j + 6)
                    if v == 4:
                        pe.wait_ge(s_raw_done, RAWS * j + 7)
                        pe.wait_ge(s_yraw, 2 * j + 1)
                    pe.wait_ge(s_alo, 16 * j + 8 + v + 1)
                    cols = slice(i * P, (i + 1) * P)
                    ins = split3(ybank[:, i * P:SEQ], hi[:, T_RV + hd, cols], lo[:, T_RV + hd, cols],
                                 hi[:, T_A + v % 2, 0:width(i)], lo[:, T_A + v % 2, 0:width(i)],
                                 start=(i == 0), stop=(i == 3), skip=True)
                    if i == 3:
                        ins.then_inc(s_yr, 1)

            def free_bank(j, s):
                pe.wait_ge(s_evac, SLOTS * j + s - 2)

            def front(j, prev):
                for s in range(3):
                    hooks = {}
                    if prev is not None:
                        free_bank(j, s)
                        hooks = {1: lambda: r_step(prev, 3 * s), 4: lambda: r_step(prev, 3 * s + 1),
                                 7: lambda: r_step(prev, 3 * s + 2)}
                    if s == 0 and prev is not None:
                        hooks[5] = lambda: turn_v(prev, 8, (s_raw_done, RAWS * j - 1))
                    if s == 1:
                        hooks[5] = lambda: stat_qk(j, 0, None if prev is None else (s_raw_done, RAWS * j))
                    if s == 2:
                        hooks[3] = lambda: stat_qk(j, 1, (s_misc, 1 if prev is None else 4 * j - 1))
                        if prev is not None:
                            hooks[6] = lambda: stat_y(prev, 0, (s_misc, 4 * j))
                    before = {k: (s_h, k + 1) for k in range(KD)} if prev is None and s == 0 else None
                    chunk(SLOTS * j + s, s % RING, s % 3, KD, T_H, hooks, before=before)

            def back(j, prev):
                for s in range(3, SLOTS):
                    free_bank(j, s)
                    hooks = {3: lambda: sb_step(j, 2 * (s - 3))}
                    if s < 8:
                        hooks[7] = lambda: sb_step(j, 2 * (s - 3) + 1)
                    if s == 3:
                        if prev is not None:
                            hooks[2] = lambda: stat_y(prev, 1, (s_misc, 4 * j + 1))
                        hooks[5] = lambda: turn_v(j, 2, (s_misc, 4 * j + 2))
                    if s == 8:
                        hooks = {5: lambda: sb_step(j, 10), 6: lambda: turn_v(j, 7, (s_raw_done, RAWS * j + 5))}
                    chunk(SLOTS * j + s, s % RING, s % 3, KD, T_H, hooks)

            front(0, None)
            back(0, None)
            with pe.Fori(1, PAIRS) as j:
                front(j, j - 1)
                back(j, j - 1)

            last = PAIRS - 1
            for s in range(3):
                free_bank(PAIRS, s)
                hooks = {1: lambda: r_step(last, 3 * s), 4: lambda: r_step(last, 3 * s + 1),
                         7: lambda: r_step(last, 3 * s + 2)}
                if s == 0:
                    hooks[5] = lambda: turn_v(last, 8, (s_raw_done, RAWS * PAIRS - 1))
                if s == 2:
                    hooks[3] = lambda: stat_y(last, 0, (s_raw_done, RAWS * PAIRS))
                chunk(GATE0 + s, s, s, KD, T_H, hooks)
            pe.wait_ge(s_gate, 1)
            chunk(GATE0 + 3, 0, 0, KD, T_H, {3: lambda: stat_y(last, 1, (s_misc, 4 * PAIRS - 1))})

            def branch_a(c, r, m):
                chunk(c, r, r, 4, T_YS)

            def branch_b(c, r, m, before=None):
                chunk(c, r, r, KD, T_YR, before=before)

            pe.wait_ge(s_gate, 2)
            branch_a(GATE0 + 4, 1, 0)
            pe.wait_ge(s_gate, 3)
            branch_b(GATE0 + 5, 2, 0, before={6: (s_yrlo, 7), 7: (s_yrlo, 8)})
            with pe.Fori(0, 2) as it:
                for q in range(3):
                    c = MERGE0 + 12 * it + 4 * q
                    m = 3 * it + (q + 1)
                    pe.wait_ge(s_gate, 2 * m + 2)
                    chunk(c, (4 * q) % 3, (4 * q) % 3, KD, T_H)
                    pe.wait_ge(s_read, 2 * m - 1)
                    chunk(c + 1, (4 * q + 1) % 3, (4 * q + 1) % 3, KD, T_H)
                    pe.wait_ge(s_read, 2 * m)
                    branch_a(c + 2, (4 * q + 2) % 3, m)
                    pe.wait_ge(s_gate, 2 * m + 3)
                    branch_b(c + 3, (4 * q + 3) % 3, m)
            pe.wait_ge(s_gate, 16)
            branch_a(OUT0 - 2, 0, 7)
            pe.wait_ge(s_read, 13)
            branch_b(OUT0 - 1, 1, 7)

            def tile(t, b, c, r, kt, tile0, **kw):
                pe.wait_ge(s_read, read(t) - 3)
                chunk(c, r, b, kt, tile0, **kw)

            def out_tile(m, b, **kw):
                tile(OUT0 + m, b, OUT0 + m, b, KD, T_M, **kw)

            out_tile(0, OUT0 % 3, before={k: (s_mlo, k + 1) for k in range(KD)})
            with pe.Fori(0, 2) as it:
                for q in range(3):
                    out_tile(3 * it + (q + 1), (OUT0 + q + 1) % 3)
            out_tile(7, (OUT0 + 7) % 3)

            def stat_res(n):
                pe.wait_ge(s_acc, KD * n)
                stat(C_ONES, A_ACC, s_rst)

            def up(u, b, **kw):
                tile(UP0 + u, b, UP0 + u, b, KD, T_H, **kw)

            up(0, UP0 % 3, hooks={7: lambda: stat_res(1)}, before={k: (s_relo, k + 1) for k in range(KD)})
            up(1, (UP0 + 1) % 3)
            with pe.Fori(0, 7) as it:
                for q in range(6):
                    up(6 * it + (q + 2), (UP0 + 2 + q) % 3)

            def down(m, b, before=None):
                pe.wait_ge(s_read, read(DOWN0 + m) - 3)
                for t in range(3):
                    k0 = sum(DOWN_K[:t])
                    chunk(DOWN0 + 3 * m + t, t, b, DOWN_K[t], T_G + k0, k_first=k0, last=(t == 2),
                          before=before if t == 2 else None)

            down(0, 0, before={DOWN_K[2] - 2: (s_glo, FB - 1), DOWN_K[2] - 1: (s_glo, FB)})
            with pe.Fori(0, 2) as it:
                for q in range(3):
                    down(3 * it + (q + 1), (q + 1) % 3)
            down(7, 7 % 3)

            def ple(m, q, **kw):
                t = PLET0 + 2 * m
                c = PLE0 + 2 * m
                tile(t, (PLET0 + 2 * q) % 3, c, (2 * q) % 3, KD, T_H, **kw)
                tile(t + 1, (PLET0 + 2 * q + 1) % 3, c + 1, (2 * q + 1) % 3, PB, T_P)

            pe.wait_ge(s_plo, 1)
            ple(0, 0, hooks={7: lambda: stat_res(2)}, before={k: (s_relo, KD + k + 1) for k in range(KD)})
            with pe.Fori(0, 2) as it:
                for q in range(3):
                    ple(3 * it + (q + 1), q + 1)
            ple(7, 7)

        @block.scalar
        def _(act):
            def run(out, src, func, done, **kw):
                return nc.scalar.activation(out, src, func, **kw).then_inc(done, 1)

            def ln_exp_tables():
                nc.scalar.preload_act_table_set("natural_log_exp_and_others")

            act.dma_start(cst[:, :, :], consts).then_inc(s_cst, 16)
            for col, src, n in ((G_MIX, g_mix, 8), (G_FFN, g_ffn, 8), (G_PLE, g_ple, 8), (G_RET, g_ret, 8),
                                (G_SBQ, g_sbq, 4), (G_SBK, g_sbk, 4)):
                act.dma_start(gain[:, col:col + n, 0], src).then_inc(s_gain, 16)
            act.dma_start(cw[:, 0:3, :, 0], conv_w).then_inc(s_cw, 16)
            act.dma_start(cw[:, 3, :, 0], conv_b).then_inc(s_cw, 16)
            act.wait_ge(s_eps, 1)
            ln_exp_tables()

            def high(third, r, kt=8, first=False):
                act.wait_ge(s_wdma[r], 16 * (third + 1))
                if not first:
                    act.wait_ge(s_used, 3 * third + r - 2)
                nc.scalar.copy(w_hi[r][:, 0:kt, :], w_f[r][:, 0:kt, :]).then_inc(s_whi, 1)

            for k in range(KD):
                if k % 2 == 0:
                    act.wait_ge(s_x[k // 2], 16)
                if k >= 4:
                    act.wait_ge(s_xst, k - 3)
                run(fs[:, A_T + k % 4, :], fs[:, A_X + k, :], ACT.Square, s_xsq)
            act.wait_ge(s_xst, KD)
            run(fs[:, A_RS, :], misc[:, :], ACT.Ln, s_xln, scale=1.0 / D, bias=eps[:, :])
            act.wait_ge(s_xln, 1)
            run(fs[:, A_RS, :], fs[:, A_RS, :], ACT.Exp, s_xrs, scale=-0.5)
            high(0, 0, first=True)
            for k in range(KD):
                act.wait_ge(s_hf, k + 1)
                nc.scalar.copy(hi[:, T_H + k, :], fs[:, A_X + k, :]).then_inc(s_hhi, 1)
                if k == 3:
                    high(0, 1, first=True)

            def evac(j, s):
                act.wait_ge(s_used, SLOTS * j + s + 1)
                static0 = isinstance(j, int) and j == 0
                if s in RAW_OF:
                    n = RAW_OF[s]
                    if n >= 2 or not static0:
                        act.wait_ge(s_raw_done, RAWS * j + n - (1 if n else 0))
                    dst = fs[:, A_RAW + n % 2, :]
                else:
                    if s == 5 and not static0:
                        act.wait_ge(s_yf, 2 * j)
                    dst = fs[:, A_G + s - 5, :]
                nc.scalar.copy(dst, bank[s % 3][:, :]).then_inc(s_evac, 1)

            def norm_qk(j, t, free):
                act.wait_ge(s_stat, 2 * j + t + 1)
                run(fs[:, A_SQ, :], misc[:, :], ACT.Ln, s_misc, scale=1.0 / 64, bias=eps[:, :])
                act.wait_ge(s_misc, free)
                run(fs[:, A_SQ, :], fs[:, A_SQ, :], ACT.Exp, s_rs, scale=-0.5)

            def norm_y(j, hd, free):
                act.wait_ge(s_ystat, 2 * j + hd + 1)
                run(fs[:, A_SQY[hd], :], misc[:, :], ACT.Ln, s_misc, scale=1.0 / P, bias=eps[:, :])
                act.wait_ge(s_misc, free)
                run(fs[:, A_SQY[hd], :], fs[:, A_SQY[hd], :], ACT.Exp, s_yrs, scale=-0.5)

            def high_qk(j, t):
                act.wait_ge(s_nrm, 2 * j + t + 1)
                nc.scalar.copy(hi[:, T_SBQ + t, :], fs[:, A_RAW + t, :]).then_inc(s_nhi, 1)

            def high_rot(j, t):
                act.wait_ge(s_rot, 2 * j + t + 1)
                nc.scalar.copy(hi[:, T_RQ + t, :], fs[:, A_RAW + (3 + t) % 2, :]).then_inc(s_rhi, 1)

            def high_v(j, n):
                act.wait_ge(s_vt, 3 * j + n + 1)
                nc.scalar.copy(hi[:, (T_SBV, T_RV, T_RV + 1)[n], :], misc[:, :]).then_inc(s_vhi, 1)

            def high_y(j, hd):
                act.wait_ge(s_yf, 2 * j + hd + 1)
                nc.scalar.copy(hi[:, T_YR + hd + 2 * j, :], fs[:, A_Y + hd, :]).then_inc(s_yrhi, 1)

            def r_high(j, n):
                _, i = r_unit(n)
                act.wait_ge(s_zd, 8 * j + n + 1)
                nc.scalar.copy(hi[:, T_A + n % 2, 0:width(i)], fs[:, A_A + n % 2, 0:width(i)]).then_inc(s_ahi, 1)

            def y_raw(j, hd):
                act.wait_ge(s_yr, 2 * j + hd + 1)
                nc.scalar.copy(fs[:, A_Y + hd, :], ybank[:, :]).then_inc(s_yraw, 1)

            def y_square(j, hd):
                act.wait_ge(s_yraw, 2 * j + hd + 1)
                run(fs[:, A_SQY[hd], :], fs[:, A_Y + hd, :], ACT.Square, s_ysq)

            def silu(j):
                act.wait_ge(s_evac, SLOTS * j + 7)
                g = fs[:, A_G:A_G + 2, :]
                run(g, g, ACT.Silu, s_silu)
                ln_exp_tables()

            def sb_step(j, n):
                u = n - 2
                if 2 <= n < 10:
                    N = width(sb_unit(u)[1])
                    act.wait_ge(s_u, 8 * j + u + 1)
                    run(fs[:, A_A + u % 2, 0:N], zbank[u % 3][:, 0:N], ACT.Exp, s_zx)
                if n < 8:
                    _, i = sb_unit(n)
                    t = fs[:, A_T + n % 2, 0:width(i)]
                    act.wait_ge(s_abs, 8 * j + n + 1)
                    run(t, t, ACT.Exp, s_e, scale=-1.0)
                    act.wait_ge(s_e, 8 * j + n + 1)
                    run(t, t, ACT.Ln, s_l, bias=1.0)
                if 2 <= n < 10:
                    act.wait_ge(s_zx, 8 * j + u + 1)
                    nc.scalar.copy(hi[:, T_A + u % 2, 0:N], fs[:, A_A + u % 2, 0:N]).then_inc(s_ahi, 1)
                if n < 8:
                    hd, i = sb_unit(n)
                    act.wait_ge(s_sp, 8 * j + n + 1)
                    if n >= 5:
                        act.wait_ge(s_u, 8 * j + 4)
                    nc.scalar.copy(sp_view(hi, hd, i), fs[:, A_T + n % 2, 0:width(i)]).then_inc(s_sphi, 1)
                if n in (6, 10):
                    hd = (n - 6) // 4
                    rows = slice(64 * hd, 64 * hd + 64)
                    act.wait_ge(s_ysum, 2 * j + hd + 1)
                    nc.scalar.copy(hi[rows, T_YS + j, :], ybank[rows, :]).then_inc(s_yshi, 1)

            def ahead(j, s):
                q = s + 2
                high(3 * j + q // 3, q % 3)

            def front(j, prev):
                if prev is not None:
                    evac(prev, 8)
                    r_high(prev, 0)
                ahead(j, 0)
                if prev is not None:
                    r_high(prev, 1)
                    high_v(prev, 2)
                    r_high(prev, 2)
                ahead(j, 1)
                evac(j, 0)
                if prev is not None:
                    r_high(prev, 3)
                    y_raw(prev, 0)
                    r_high(prev, 4)
                norm_qk(j, 0, 1 if prev is None else 4 * j - 1)
                if prev is not None:
                    r_high(prev, 5)
                    y_square(prev, 0)
                evac(j, 1)
                if prev is not None:
                    r_high(prev, 6)
                high_qk(j, 0)
                ahead(j, 2)
                norm_qk(j, 1, 2 if prev is None else 4 * j)
                if prev is not None:
                    r_high(prev, 7)
                    y_raw(prev, 1)
                    y_square(prev, 1)

            def back(j, prev):
                high_qk(j, 1)
                evac(j, 2)
                if prev is not None:
                    norm_y(prev, 0, 4 * j + 1)
                ahead(j, 3)
                if prev is not None:
                    norm_y(prev, 1, 4 * j + 2)
                sb_early(j, 0)
                high_v(j, 0)
                sb_late(j, 0)
                sb_early(j, 1)
                if prev is not None:
                    high_y(prev, 0)
                sb_late(j, 1)
                ahead(j, 4)
                evac(j, 3)
                sb_step(j, 2)
                sb_step(j, 3)
                if prev is not None:
                    high_y(prev, 1)
                ahead(j, 5)
                evac(j, 4)
                sb_step(j, 4)
                sb_step(j, 5)
                high_rot(j, 0)
                ahead(j, 6)
                evac(j, 5)
                sb_step(j, 6)
                sb_step(j, 7)
                high_rot(j, 1)
                evac(j, 6)
                ahead(j, 7)
                sb_step(j, 8)
                silu(j)
                sb_step(j, 9)
                evac(j, 7)
                ahead(j, 8)
                sb_step(j, 10)
                high_v(j, 1)

            def sb_early(j, n):
                _, i = sb_unit(n)
                t = fs[:, A_T + n % 2, 0:width(i)]
                act.wait_ge(s_abs, 8 * j + n + 1)
                run(t, t, ACT.Exp, s_e, scale=-1.0)
                act.wait_ge(s_e, 8 * j + n + 1)
                run(t, t, ACT.Ln, s_l, bias=1.0)

            def sb_late(j, n):
                hd, i = sb_unit(n)
                act.wait_ge(s_sp, 8 * j + n + 1)
                nc.scalar.copy(sp_view(hi, hd, i), fs[:, A_T + n % 2, 0:width(i)]).then_inc(s_sphi, 1)

            front(0, None)
            back(0, None)
            with act.Fori(1, PAIRS) as j:
                front(j, j - 1)
                back(j, j - 1)

            last = PAIRS - 1

            def raw_gate(n):
                act.wait_ge(s_used, GATE0 + n + 1)
                nc.scalar.copy(fs[:, A_SG[n // 2] + n % 2, :], bank[n % 3][:, :]).then_inc(s_gate, 1)

            evac(last, 8)
            r_high(last, 0)
            ahead(PAIRS, 0)
            r_high(last, 1)
            high_v(last, 2)
            r_high(last, 2)
            ahead(PAIRS, 1)
            raw_gate(0)
            r_high(last, 3)
            y_raw(last, 0)
            r_high(last, 4)
            y_square(last, 0)
            r_high(last, 5)
            high((GATE0 + 4) // 3, 1, 4)
            raw_gate(1)
            r_high(last, 6)
            r_high(last, 7)
            norm_y(last, 0, 4 * PAIRS - 1)
            y_raw(last, 1)
            y_square(last, 1)
            high((GATE0 + 5) // 3, 2)
            high_y(last, 0)
            raw_gate(2)
            norm_y(last, 1, 4 * PAIRS)
            high_y(last, 1)
            high(MERGE0 // 3, 0)
            raw_gate(3)
            for m in range(2):
                act.wait_ge(s_gate, 2 * m + 2)
                g = fs[:, A_SG[m]:A_SG[m] + 2, :]
                run(g, g, ACT.Sigmoid, s_sig)
            high(MERGE0 // 3, 1)
            act.wait_ge(s_yrlo, 8)
            act.dma_start(fs[:, A_X:A_X + 8, :], xT).then_inc(s_xt, 16)

            def high_merged(m, ring):
                act.wait_ge(s_madd, m + 1)
                nc.scalar.copy(hi[:, T_M + m, :], fs[:, A_SG[ring], :]).then_inc(s_mhi, 1)

            def gate(c, q, t):
                act.wait_ge(s_used, c + t + 1)
                run(fs[:, A_SG[(q + 2) % 3] + t, :], bank[(4 * q + t) % 3][:, :], ACT.Sigmoid, s_gate)

            with act.Fori(0, 2) as it:
                for q in range(3):
                    c = MERGE0 + 12 * it + 4 * q
                    m = 3 * it + (q + 1)

                    def two_ahead(t, kt=8):
                        high(MERGE0 // 3 + 4 * it + (4 * q + t + 2) // 3, (4 * q + t + 2) % 3, kt)

                    two_ahead(0, 4)
                    high_merged(m - 1, q)
                    two_ahead(1)
                    gate(c, q, 0)
                    two_ahead(2)
                    gate(c, q, 1)
                    two_ahead(3)
            high(OUT0 // 3, OUT0 % 3)
            high_merged(6, 0)
            high((OUT0 + 1) // 3, (OUT0 + 1) % 3)
            high((OUT0 + 2) // 3, (OUT0 + 2) % 3)
            high_merged(7, 1)

            def residual(t, n, phase, col):
                act.wait_ge(s_read, read(t))
                x = fs[:, A_X + n, :]
                run(fs[:, A_SQR, :], x, ACT.Square, s_rsq)
                run(hi[:, T_H + n, :], x, ACT.Identity, s_rehi, scale=gain[:, col + n, :])

            def norm_res(n):
                ln_exp_tables()
                act.wait_ge(s_rst, n)
                run(fs[:, A_RS, :], misc[:, :], ACT.Ln, s_rln, scale=1.0 / D, bias=eps[:, :])
                act.wait_ge(s_rln, n)
                run(fs[:, A_RS, :], fs[:, A_RS, :], ACT.Exp, s_rrs, scale=-0.5)

            high((OUT0 + 3) // 3, (OUT0 + 3) % 3)
            residual(OUT0, 0, 0, G_FFN)
            with act.Fori(0, 2) as it:
                for q in range(3):
                    c = OUT0 + 4 + q
                    high(c // 3 + it, c % 3)
                    n = 3 * it + (q + 1)
                    residual(OUT0 + n, n, 0, G_FFN)

            def conv_gelu(f):
                act.wait_ge(s_read, read(UP0 + 2 * f))
                run(fs[:, A_C, :], fs_flat[:, A_CONV * SEQ + 2:A_CONV * SEQ + 2 + SEQ], ACT.Identity, s_c0,
                    scale=cw[:, 2, f, :], bias=cw[:, 3, f, :])
                act.wait_ge(s_c2, f + 1)
                run(fs[:, A_C, :], fs[:, A_C, :], ACT.Gelu_apprx_tanh, s_gelu)

            def high_g(f):
                act.wait_ge(s_g, f + 1)
                nc.scalar.copy(hi[:, T_G + f, :], fs[:, A_U, :]).then_inc(s_ghi, 1)

            high((UP0 + 2) // 3, (UP0 + 2) % 3)
            residual(OUT0 + 7, 7, 0, G_FFN)
            high((UP0 + 3) // 3, (UP0 + 3) % 3)
            norm_res(1)
            act.wait_ge(s_cw, 32)
            conv_gelu(0)
            act.wait_ge(s_mlo, KD)
            act.dma_start(fs[:, A_P:A_P + PB, :], pT).then_inc(s_p, 16)
            with act.Fori(0, 7) as it:
                for q in range(3):
                    c = UP0 + 4 + 2 * q
                    f = 3 * it + (q + 1)
                    high(c // 3 + 2 * it, c % 3)
                    high_g(f - 1)
                    high((c + 1) // 3 + 2 * it, (c + 1) % 3)
                    conv_gelu(f)

            def down_ahead(m, t):
                u = t + 2
                high(DOWN0 // 3 + m + u // 3, u % 3, DOWN_K[u % 3])

            down_ahead(0, 0)
            high_g(FB - 1)
            down_ahead(0, 1)
            act.wait_ge(s_p, 16)
            nc.scalar.copy(hi[:, T_P:T_P + PB, :], fs[:, A_P:A_P + PB, :]).then_inc(s_phi, 1)
            down_ahead(0, 2)
            down_ahead(1, 0)
            residual(DOWN0, 0, 1, G_PLE)
            down_ahead(1, 1)
            down_ahead(1, 2)
            with act.Fori(0, 2) as it:
                for q in range(3):
                    n = 3 * it + (q + 1)
                    down_ahead(n + 1, 0)
                    residual(DOWN0 + n, n, 1, G_PLE)
                    high(DOWN0 // 3 + n + 2, 0, 8)
                    high(DOWN0 // 3 + n + 2, 1, 8)

            def ple_ahead(c):
                if c < PLE0 + 2 * KD:
                    high(c // 3, c % 3, PB if c % 2 else 8)

            def ple_gate(m):
                act.wait_ge(s_read, read(PLET0 + 2 * m))
                run(fs[:, A_U, :], fs[:, A_U, :], ACT.Sigmoid, s_pg)

            ple_ahead(PLE0 + 2)
            residual(DOWN0 + 7, 7, 1, G_PLE)
            ple_ahead(PLE0 + 3)
            norm_res(2)
            ple_gate(0)
            for m in range(1, KD):
                ple_ahead(PLE0 + 2 * m + 2)
                ple_ahead(PLE0 + 2 * m + 3)
                ple_gate(m)

        @block.vector
        def _(dve):
            def tt(out, a, b, op, done):
                return nc.vector.tensor_tensor(out, a, b, op).then_inc(done, 1)

            def stt(out, a, scalar, b, op0, op1, done):
                return nc.vector.scalar_tensor_tensor(out=out, in0=a, scalar=scalar, in1=b, op0=op0,
                                                      op1=op1).then_inc(done, 1)

            def low(third, r, kt=8):
                dve.wait_ge(s_whi, 3 * third + r + 1)
                tt(w_lo[r][:, 0:kt, :], w_f[r][:, 0:kt, :], w_hi[r][:, 0:kt, :], ALU.subtract, s_wlo)

            nc.vector.memset(eps[:, :], EPS).then_inc(s_eps, 1)
            dve.wait_ge(s_cst, 16)
            nc.vector.tensor_copy(cr[:, :, :], cst[:, :, :]).then_inc(s_cr, 1)
            dve.wait_ge(s_gain, 16 * 6)
            g8 = gain[:, G_SBQ:G_SBQ + PAIRS, 0]
            nc.vector.tensor_scalar(g8, g8, 0.125, None, ALU.mult).then_inc(s_cr, 1)
            dve.wait_ge(s_cr, 2)

            low(0, 0)
            for k in range(KD):
                if k == 0:
                    dve.wait_ge(s_xrs, 1)
                x = fs[:, A_X + k, :]
                stt(x, x, gain[:, G_MIX + k, :], fs[:, A_RS, :], ALU.mult, ALU.mult, s_hf)
                if k >= 1:
                    dve.wait_ge(s_hhi, k)
                    tt(lo[:, T_H + k - 1, :], fs[:, A_X + k - 1, :], hi[:, T_H + k - 1, :], ALU.subtract, s_h)
            dve.wait_ge(s_hhi, KD)
            tt(lo[:, T_H + KD - 1, :], fs[:, A_X + KD - 1, :], hi[:, T_H + KD - 1, :], ALU.subtract, s_h)
            low(0, 1)
            dve.wait_ge(s_rope, 16)

            def square(j, t):
                dve.wait_ge(s_evac, SLOTS * j + t + 1)
                r = fs[:, A_RAW + t, :]
                if t == 1:
                    dve.wait_ge(s_nrm, 2 * j + 1)
                tt(fs[:, A_SQ, :], r, r, ALU.mult, s_sq)

            def norm(j, t):
                dve.wait_ge(s_rs, 2 * j + t + 1)
                r = fs[:, A_RAW + t, :]
                col = (G_SBQ, G_SBK)[t]
                stt(r, r, gain[:, col + j, :], fs[:, A_SQ, :], ALU.mult, ALU.mult, s_nrm)

            def low_qk(j, t):
                dve.wait_ge(s_nhi, 2 * j + t + 1)
                tt(lo[:, T_SBQ + t, :], fs[:, A_RAW + t, :], hi[:, T_SBQ + t, :], ALU.subtract, s_raw_done)

            def rotate(j, t):
                dve.wait_ge(s_swap, 64 * (2 * j + t + 1))
                raw, other = fs[:, A_RAW + (3 + t) % 2, :], fs[:, A_SWAP, :]
                tt(raw, raw, fs[:, A_COS, :], ALU.mult, s_rmul)
                tt(other, other, fs[:, A_COS + 1, :], ALU.mult, s_rmul)

            def rotate_sum(j, t):
                raw, other = fs[:, A_RAW + (3 + t) % 2, :], fs[:, A_SWAP, :]
                dve.wait_ge(s_rmul, 4 * j + 2 * t + 2)
                tt(raw, raw, other, ALU.add, s_rot)

            def low_rot(j, t):
                dve.wait_ge(s_rhi, 2 * j + t + 1)
                tt(lo[:, T_RQ + t, :], fs[:, A_RAW + (3 + t) % 2, :], hi[:, T_RQ + t, :], ALU.subtract, s_raw_done)

            def low_v(j, n):
                dve.wait_ge(s_vhi, 3 * j + n + 1)
                t = (T_SBV, T_RV, T_RV + 1)[n]
                nc.vector.tensor_tensor(lo[:, t, :], misc[:, :], hi[:, t, :], ALU.subtract).then_inc(s_raw_done, 1)

            def r_scores(j, n):
                hd, i = r_unit(n)
                N = width(i)
                if n == 0:
                    dve.wait_ge(s_dec, 16 * (j + 1))
                dve.wait_ge(s_zr, 8 * j + n + 1)
                tt(fs[:, A_A + n % 2, 0:N], zbank[n % 3][:, 0:N], fs[:, A_DEC + hd, 0:N], ALU.mult, s_zd)

            def r_low(j, n):
                _, i = r_unit(n)
                N = width(i)
                dve.wait_ge(s_ahi, 16 * j + 8 + n + 1)
                tt(lo[:, T_A + n % 2, 0:N], fs[:, A_A + n % 2, 0:N], hi[:, T_A + n % 2, 0:N], ALU.subtract, s_alo)

            def y_norm(j, hd):
                dve.wait_ge(s_yrs, 2 * j + hd + 1)
                y = fs[:, A_Y + hd, :]
                col = G_RET + hd + 2 * j
                stt(y, y, gain[:, col, :], fs[:, A_SQY[hd], :], ALU.mult, ALU.mult, s_yn)

            def y_swish(j, hd):
                y = fs[:, A_Y + hd, :]
                dve.wait_ge(s_silu, j + 1)
                dve.wait_ge(s_yn, 2 * j + hd + 1)
                tt(y, y, fs[:, A_G + hd, :], ALU.mult, s_yf)

            def low_y(j, hd):
                dve.wait_ge(s_yrhi, 2 * j + hd + 1)
                t = T_YR + hd + 2 * j
                tt(lo[:, t, :], fs[:, A_Y + hd, :], hi[:, t, :], ALU.subtract, s_yrlo)

            def sb_abs(j, n):
                N = width(sb_unit(n)[1])
                dve.wait_ge(s_z, 8 * j + n + 1)
                nc.vector.tensor_scalar(fs[:, A_T + n % 2, 0:N].bitcast(I32), zbank[n % 3][:, 0:N].bitcast(I32),
                                        0x7FFFFFFF, None, ALU.bitwise_and).then_inc(s_abs, 1)

            def sb_softplus(j, n):
                N = width(sb_unit(n)[1])
                t = fs[:, A_T + n % 2, 0:N]
                dve.wait_ge(s_l, 8 * j + n + 1)
                stt(t, zbank[n % 3][:, 0:N], 0.0, t, ALU.max, ALU.add, s_sp)

            def sb_low(j, n):
                hd, i = sb_unit(n)
                dve.wait_ge(s_sphi, 8 * j + n + 1)
                tt(sp_view(lo, hd, i), fs[:, A_T + n % 2, 0:width(i)], sp_view(hi, hd, i), ALU.subtract, s_splo)

            def sb_step(j, n, beside=None, after=None):
                if n < 8:
                    sb_abs(j, n)
                    if beside:
                        beside()
                    sb_softplus(j, n)
                if 2 <= n < 10:
                    u = n - 2
                    N = width(sb_unit(u)[1])
                    dve.wait_ge(s_ahi, 16 * j + u + 1)
                    tt(lo[:, T_A + u % 2, 0:N], fs[:, A_A + u % 2, 0:N], hi[:, T_A + u % 2, 0:N], ALU.subtract,
                       s_alo)
                if after:
                    after()
                if n < 8:
                    sb_low(j, n)
                if n in (6, 10):
                    hd = (n - 6) // 4
                    rows = slice(64 * hd, 64 * hd + 64)
                    dve.wait_ge(s_yshi, 2 * j + hd + 1)
                    tt(lo[rows, T_YS + j, :], ybank[rows, :], hi[rows, T_YS + j, :], ALU.subtract, s_yslo)

            def ahead(j, s):
                q = s + 2
                low(3 * j + q // 3, q % 3)

            def front(j, prev):
                if prev is not None:
                    r_scores(prev, 0)
                    r_low(prev, 0)
                ahead(j, 0)
                if prev is not None:
                    r_scores(prev, 1)
                    r_low(prev, 1)
                    low_v(prev, 2)
                    r_scores(prev, 2)
                    r_low(prev, 2)
                ahead(j, 1)
                if prev is not None:
                    r_scores(prev, 3)
                square(j, 0)
                if prev is not None:
                    r_low(prev, 3)
                    r_scores(prev, 4)
                    r_low(prev, 4)
                    r_scores(prev, 5)
                norm(j, 0)
                if prev is not None:
                    r_low(prev, 5)
                    r_scores(prev, 6)
                square(j, 1)
                if prev is not None:
                    r_low(prev, 6)
                low_qk(j, 0)
                ahead(j, 2)
                if prev is not None:
                    r_scores(prev, 7)
                norm(j, 1)
                if prev is not None:
                    r_low(prev, 7)

            def back(j, prev):
                low_qk(j, 1)
                ahead(j, 3)
                sb_abs(j, 0)
                if prev is not None:
                    y_norm(prev, 0)
                sb_softplus(j, 0)
                low_v(j, 0)
                sb_low(j, 0)
                sb_abs(j, 1)
                if prev is not None:
                    y_swish(prev, 0)
                sb_softplus(j, 1)
                sb_low(j, 1)
                if prev is not None:
                    low_y(prev, 0)
                ahead(j, 4)
                if prev is not None:
                    sb_step(j, 2, lambda: y_norm(prev, 1), lambda: y_swish(prev, 1))
                    sb_step(j, 3, None, lambda: low_y(prev, 1))
                else:
                    sb_step(j, 2)
                    sb_step(j, 3)
                ahead(j, 5)
                sb_step(j, 4, lambda: rotate(j, 0), lambda: rotate_sum(j, 0))
                sb_step(j, 5)
                low_rot(j, 0)
                ahead(j, 6)
                sb_step(j, 6, lambda: rotate(j, 1), lambda: rotate_sum(j, 1))
                sb_step(j, 7)
                low_rot(j, 1)
                ahead(j, 7)
                sb_step(j, 8)
                sb_step(j, 9)
                ahead(j, 8)
                sb_step(j, 10)
                low_v(j, 1)

            front(0, None)
            back(0, None)
            with dve.Fori(1, PAIRS) as j:
                front(j, j - 1)
                back(j, j - 1)

            last = PAIRS - 1
            r_scores(last, 0)
            r_low(last, 0)
            ahead(PAIRS, 0)
            r_scores(last, 1)
            r_low(last, 1)
            low_v(last, 2)
            r_scores(last, 2)
            r_low(last, 2)
            ahead(PAIRS, 1)
            for n in range(3, 6):
                r_scores(last, n)
                r_low(last, n)
            low((GATE0 + 4) // 3, 1, 4)
            for n in range(6, 8):
                r_scores(last, n)
                r_low(last, n)
            y_norm(last, 0)
            y_swish(last, 0)
            low((GATE0 + 5) // 3, 2)
            low_y(last, 0)
            y_norm(last, 1)
            y_swish(last, 1)
            low_y(last, 1)

            def branch(m, t, used, b, ring):
                g = fs[:, A_SG[ring] + t, :]
                dve.wait_ge(s_used, used)
                tt(g, bank[b][:, :], g, ALU.mult, s_read)

            def merge(m, ring):
                g0, g1 = fs[:, A_SG[ring], :], fs[:, A_SG[ring] + 1, :]
                dve.wait_ge(s_read, 2 * m + 2)
                tt(g0, g0, g1, ALU.add, s_madd)

            def low_merged(m, ring):
                dve.wait_ge(s_mhi, m + 1)
                tt(lo[:, T_M + m, :], fs[:, A_SG[ring], :], hi[:, T_M + m, :], ALU.subtract, s_mlo)

            low(MERGE0 // 3, 0)
            low(MERGE0 // 3, 1)
            dve.wait_ge(s_sig, 1)
            branch(0, 0, GATE0 + 5, 1, 0)
            with dve.Fori(0, 2) as it:
                for q in range(3):
                    c = MERGE0 + 12 * it + 4 * q
                    m = 3 * it + (q + 1)

                    def two_ahead(t, kt=8):
                        low(MERGE0 // 3 + 4 * it + (4 * q + t + 2) // 3, (4 * q + t + 2) % 3, kt)

                    two_ahead(0, 4)
                    branch(m - 1, 1, c, (4 * q + 2) % 3, q)
                    merge(m - 1, q)
                    two_ahead(1)
                    low_merged(m - 1, q)
                    two_ahead(2)
                    two_ahead(3)
                    dve.wait_ge(s_gate, 2 * m + 2)
                    branch(m, 0, c + 3, (4 * q + 2) % 3, (q + 1) % 3)
            low(OUT0 // 3, OUT0 % 3)
            branch(6, 1, OUT0 - 2, 2, 0)
            merge(6, 0)
            low((OUT0 + 1) // 3, (OUT0 + 1) % 3)
            low_merged(6, 0)
            dve.wait_ge(s_gate, 16)
            branch(7, 0, OUT0 - 1, 0, 1)
            low((OUT0 + 2) // 3, (OUT0 + 2) % 3)
            branch(7, 1, OUT0, 1, 1)
            merge(7, 1)
            low_merged(7, 1)

            def residual(n, phase, col, used, b):
                x = fs[:, A_X + n, :]
                dve.wait_ge(s_used, used)
                tt(x, x, bank[b][:, :], ALU.add, s_read)
                at = KD * phase + n + 1
                dve.wait_ge(s_rehi, at)
                stt(lo[:, T_H + n, :], x, gain[:, col + n, :], hi[:, T_H + n, :], ALU.mult, ALU.subtract,
                    s_relo)
                dve.wait_ge(s_rsq, at)
                acc, sq = fs[:, A_ACC, :], fs[:, A_SQR, :]
                if isinstance(n, int) and n == 0:
                    nc.vector.tensor_copy(acc, sq).then_inc(s_acc, 1)
                else:
                    dve.wait_ge(s_acc, at - 1)
                    tt(acc, acc, sq, ALU.add, s_acc)

            low((OUT0 + 3) // 3, (OUT0 + 3) % 3)
            dve.wait_ge(s_xt, 16)
            residual(0, 0, G_FFN, OUT0 + 1, OUT0 % 3)
            with dve.Fori(0, 2) as it:
                for q in range(3):
                    c = OUT0 + 4 + q
                    low(c // 3 + it, c % 3)
                    n = 3 * it + (q + 1)
                    residual(n, 0, G_FFN, OUT0 + n + 1, (OUT0 + q + 1) % 3)

            a_pad = fs_flat[:, A_CONV * SEQ:A_CONV * SEQ + SEQ + 2]
            cv, rs = fs[:, A_C, :], fs[:, A_RS, :]

            def gate_path(f, b):
                dve.wait_ge(s_used, UP0 + 2 * f + 1)
                tt(a_pad[:, 2:], bank[b][:, :], rs, ALU.mult, s_read)
                dve.wait_ge(s_c0, f + 1)
                stt(cv, a_pad[:, 1:SEQ + 1], cw[:, 1, f, :], cv, ALU.mult, ALU.add, s_c1)
                dve.wait_ge(s_c1, f + 1)
                stt(cv, a_pad[:, 0:SEQ], cw[:, 0, f, :], cv, ALU.mult, ALU.add, s_c2)

            def value_path(f, b):
                u = fs[:, A_U, :]
                dve.wait_ge(s_used, UP0 + 2 * f + 2)
                tt(u, bank[b][:, :], rs, ALU.mult, s_read)
                dve.wait_ge(s_gelu, f + 1)
                dve.wait_ge(s_read, read(UP0 + 1 + 2 * f))
                tt(u, u, cv, ALU.mult, s_g)
                dve.wait_ge(s_ghi, f + 1)
                tt(lo[:, T_G + f, :], u, hi[:, T_G + f, :], ALU.subtract, s_glo)

            low((UP0 + 2) // 3, (UP0 + 2) % 3)
            residual(7, 0, G_FFN, OUT0 + 8, (OUT0 + 7) % 3)
            nc.vector.memset(a_pad[:, 0:2], 0.0).then_inc(s_halo, 1)
            dve.wait_ge(s_halo, 1)
            low((UP0 + 3) // 3, (UP0 + 3) % 3)
            dve.wait_ge(s_rrs, 1)
            gate_path(0, UP0 % 3)
            with dve.Fori(0, 7) as it:
                for q in range(3):
                    c = UP0 + 4 + 2 * q
                    f = 3 * it + (q + 1)
                    low(c // 3 + 2 * it, c % 3)
                    value_path(f - 1, (UP0 + 1 + 2 * q) % 3)
                    low((c + 1) // 3 + 2 * it, (c + 1) % 3)
                    gate_path(f, (UP0 + 2 + 2 * q) % 3)

            def down_ahead(m, t):
                u = t + 2
                low(DOWN0 // 3 + m + u // 3, u % 3, DOWN_K[u % 3])

            down_ahead(0, 0)
            value_path(FB - 1, (DOWN0 - 1) % 3)
            down_ahead(0, 1)
            dve.wait_ge(s_phi, 1)
            tt(lo[:, T_P:T_P + PB, :], fs[:, A_P:A_P + PB, :], hi[:, T_P:T_P + PB, :], ALU.subtract, s_plo)
            down_ahead(0, 2)
            down_ahead(1, 0)
            residual(0, 1, G_PLE, DOWN0 + 3, DOWN0 % 3)
            down_ahead(1, 1)
            down_ahead(1, 2)
            with dve.Fori(0, 2) as it:
                for q in range(3):
                    n = 3 * it + (q + 1)
                    down_ahead(n + 1, 0)
                    residual(n, 1, G_PLE, DOWN0 + 3 * n + 3, (DOWN0 + q + 1) % 3)
                    low(DOWN0 // 3 + n + 2, 0, 8)
                    low(DOWN0 // 3 + n + 2, 1, 8)

            def ple_ahead(c):
                if c < PLE0 + 2 * KD:
                    low(c // 3, c % 3, PB if c % 2 else 8)

            t = fs[:, A_U, :]

            def ple_gate(m):
                dve.wait_ge(s_used, PLE0 + 2 * m + 1)
                if m >= 1:
                    dve.wait_ge(s_y, m)
                tt(t, bank[(PLET0 + 2 * m) % 3][:, :], rs, ALU.mult, s_read)

            def ple_out(m):
                x = fs[:, A_X + m, :]
                dve.wait_ge(s_pg, m + 1)
                dve.wait_ge(s_used, PLE0 + 2 * m + 2)
                tt(t, bank[(PLET0 + 2 * m + 1) % 3][:, :], t, ALU.mult, s_read)
                dve.wait_ge(s_read, read(PLET0 + 2 * m + 1))
                tt(x, x, t, ALU.add, s_y)

            ple_ahead(PLE0 + 2)
            residual(7, 1, G_PLE, PLE0, (DOWN0 + 7) % 3)
            ple_ahead(PLE0 + 3)
            dve.wait_ge(s_rrs, 2)
            ple_gate(0)
            for m in range(1, KD):
                ple_ahead(PLE0 + 2 * m + 2)
                ple_out(m - 1)
                ple_ahead(PLE0 + 2 * m + 3)
                ple_gate(m)
            ple_out(KD - 1)


def _chunks(w):
    k, n = w.shape
    return w.reshape(k // P, P, n // P, P).transpose(2, 1, 0, 3)


def _constants(np):
    i = np.arange(P)
    consts = np.zeros((P, N_CONST, P), np.float32)
    consts[:, C_ONES] = 1.0
    consts[:, C_BLOCK] = (i[:, None] // 64 == i[None, :] // 64)
    consts[:, C_IDENT] = np.eye(P)
    consts[:, C_NEGU] = -1.0 * (i[:, None] >= i[None, :])
    consts[:, C_NEG1] = -1.0
    consts[:, C_MASK] = np.where(i[:, None] >= i[None, :], -1e30, 0.0)
    heads = np.arange(2 * PAIRS)
    log_gamma = np.log1p(-np.exp2(-5.0 - heads))
    diff = np.arange(SEQ)[None, :] - i[:, None]
    decay = np.where(diff >= 0, np.exp(np.maximum(diff, 0)[None] * log_gamma[:, None, None]), 0.0) * 64 ** -0.5
    decay = decay.reshape(PAIRS, 2, P, SEQ).transpose(0, 2, 1, 3).astype(np.float32)
    half = i % 32
    inv = (np.float32(10000.0) ** (-half.astype(np.float32) * np.float32(2.0) / np.float32(64))).astype(np.float32)
    ang = (np.arange(SEQ, dtype=np.float32)[None, :] * inv[:, None]).astype(np.float64)
    sign = np.where(i % 64 < 32, -1.0, 1.0)[:, None]
    rope = np.stack([np.cos(ang), sign * np.sin(ang)], axis=1).astype(np.float32)
    return consts, decay, rope


def kernel(**inputs):
    import numpy as np
    import concourse.bacc as bacc
    from concourse.bass_utils import run_bass_kernel_spmd as run

    a = {name: np.asarray(value) for name, value in inputs.items()}
    blocks = _chunks(a["w_in"][0])
    order = []
    for j in range(PAIRS):
        order += [j, 4 + j, 8 + j, 12 + j, 16 + j, 28 + 2 * j, 29 + 2 * j, 20 + 2 * j, 21 + 2 * j]
    for m in range(KD):
        order += [36 + m, 44 + m]
    ups = _chunks(a["w_up"][0])
    up_order = [x for f in range(FB) for x in (f, FB + f)]
    consts, decay, rope = _constants(np)

    def cols(v, n):
        return v.reshape(n, P).T

    laid = {
        "xT": a["x"][0].T.reshape(KD, P, SEQ).transpose(1, 0, 2),
        "pT": a["p"][0, 0].T.reshape(PB, P, SEQ).transpose(1, 0, 2),
        "w_in": blocks[order], "w_a": _chunks(a["w_branch_sb"][0]), "w_b": _chunks(a["w_branch_ret"][0]),
        "w_out": _chunks(a["w_out"][0]), "w_up": ups[up_order], "w_down": _chunks(a["w_down"][0]),
        "w_pg": _chunks(a["w_ple_gate"][0]), "w_pp": _chunks(a["w_ple_proj"][0]),
        "g_mix": cols(a["g_mix"], KD), "g_ffn": cols(a["g_ffn"], KD), "g_ple": cols(a["g_ple"], KD),
        "g_ret": cols(a["ret_norm_gain"], 8), "g_sbq": cols(a["sb_q_gain"], PAIRS),
        "g_sbk": cols(a["sb_k_gain"], PAIRS),
        "conv_w": a["conv_w"][0].reshape(3, FB, P).transpose(2, 0, 1), "conv_b": cols(a["conv_b"], FB),
        "consts": consts, "decay": decay, "rope": rope,
    }
    nc = bacc.Bacc("TRN2", target_bir_lowering=False, num_devices=1)
    arrays, args = {}, []
    for name, value in laid.items():
        value = np.ascontiguousarray(value)
        arrays[f"in_{name}"] = value
        args.append(nc.dram_tensor(f"in_{name}", value.shape, mybir.dt.from_np(value.dtype), kind="ExternalInput").ap())
    args.append(nc.dram_tensor("out_t", (KD, P, SEQ), F32, kind="ExternalOutput").ap())
    build(nc, *args)
    got = run(nc, [arrays], core_ids=[0]).results[0]["out_t"]
    return np.ascontiguousarray(np.asarray(got).reshape(D, SEQ).T[None])
```

```python
from contextlib import ExitStack

import concourse.bass as bass
from concourse import mybir

F32 = mybir.dt.float32
F32R = mybir.dt.float32r
I32 = mybir.dt.int32
ALU = mybir.AluOpType
ACT = mybir.ActivationFunctionType

P = 128
SEQ = 512
D = 1024
KD = D // P
NT = SEQ // P
PAIRS = 4
FB = 2816 // P
PB = 256 // P
EPS = 1e-6
RING = 3

SLOTS = 9
RAW_OF = {0: 0, 1: 1, 2: 2, 3: 3, 4: 4, 7: 5, 8: 6}
RAWS = 7
RAW_X = 8

GATE0 = PAIRS * SLOTS
MERGE0 = GATE0 + 6
OUT0 = MERGE0 + 4 * 6 + 2
UP0 = OUT0 + KD
DOWN0 = UP0 + 2 * FB
DOWN_K = (8, 8, 6)
PLE0 = DOWN0 + 3 * KD
PLET0 = DOWN0 + KD

T_H, T_YR, T_YS = 0, 8, 16
T_SBQ, T_SBK, T_SBV = 20, 21, 22
T_RQ, T_RK, T_RV = 23, 24, 25
T_SP, T_A = 27, 30
T_YQ = (28, 27)
T_X0 = 8
T_M = 20
T_G = 8
T_P = 30
N_TILES = 32

A_X = 0
A_RAW, A_SQ, A_SQY, A_SWAP, A_Y = 0, 2, (7, 3), 4, 5
A_DEC, A_COS, A_G, A_T, A_A = 8, 10, 12, 14, 16
A_SG = (10, 14, 8)
A_RS, A_ACC, A_CONV, A_C, A_SQR, A_U = 8, 9, 10, 12, 13, 16
A_RS2 = 6
A_P = 14
N_F32 = 18
H_ORDER = (0, 1, 2, 6, 4, 3, 5, 7)

C_ONES, C_BLOCK, C_IDENT, C_NEGU, C_NEG1, C_MASK = range(6)
N_CONST = 6
G_MIX, G_FFN, G_PLE, G_RET, G_SBQ, G_SBK = 0, 8, 16, 24, 32, 36
N_GAIN = 40


def build(nc, xT, pT, w_in, w_a, w_b, w_out, w_up, w_down, w_pg, w_pp, g_mix, g_ffn, g_ple, g_ret, g_sbq, g_sbk,
          conv_w, conv_b, consts, decay, rope, outT):
    with ExitStack() as ctx:
        def sb(name, shape, dt):
            return ctx.enter_context(nc.sbuf_tensor(name, shape, dt))

        def sem(name):
            return ctx.enter_context(nc.semaphore(name))

        hi = sb("hi", [P, N_TILES, SEQ], F32R)
        lo = sb("lo", [P, N_TILES, SEQ], F32R)
        fs = sb("fs", [P, N_F32, SEQ], F32)
        fs_flat = fs[:, :, :].rearrange("p t n -> p (t n)")
        w_f = [sb(f"w_f{r}", [P, 8, P], F32) for r in range(RING)]
        w_hi = [sb(f"w_hi{r}", [P, 8, P], F32R) for r in range(RING)]
        w_lo = [sb(f"w_lo{r}", [P, 8, P], F32R) for r in range(RING)]
        cst = sb("cst", [P, N_CONST, P], F32)
        cr = sb("cr", [P, N_CONST, P], F32R)
        gain = sb("gain", [P, N_GAIN, 1], F32)
        cw = sb("cw", [P, 4, FB, 1], F32)
        eps = sb("eps", [P, 1], F32)

        bank = [ctx.enter_context(nc.psum_tensor(f"dense{b}", [P, SEQ], F32)) for b in range(3)]
        zbank = [ctx.enter_context(nc.psum_tensor(f"z{b}", [P, SEQ], F32)) for b in range(3)]
        ybank = ctx.enter_context(nc.psum_tensor("ybank", [P, SEQ], F32))
        misc = ctx.enter_context(nc.psum_tensor("misc", [P, SEQ], F32))

        s_wdma = [sem(f"s_wdma{r}") for r in range(RING)]
        s_whi, s_wlo, s_used = sem("s_whi"), sem("s_wlo"), sem("s_used")
        s_cst, s_gmix, s_gain, s_eps, s_cr = sem("s_cst"), sem("s_gmix"), sem("s_gain"), sem("s_eps"), sem("s_cr")
        s_x = [sem(f"s_x{i}") for i in range(4)]
        s_xsq, s_xst, s_rope, s_dec = sem("s_xsq"), sem("s_xst"), sem("s_rope"), sem("s_dec")
        s_xhi, s_xlo, s_xacc = sem("s_xhi"), sem("s_xlo"), sem("s_xacc")
        s_xln, s_xrs, s_hf, s_hhi, s_h = sem("s_xln"), sem("s_xrs"), sem("s_hf"), sem("s_hhi"), sem("s_h")
        s_evac = sem("s_evac")
        s_raw_done = sem("s_raw_done")
        s_sq, s_stat, s_rs, s_nrm, s_nhi = sem("s_sq"), sem("s_stat"), sem("s_rs"), sem("s_nrm"), sem("s_nhi")
        s_vt, s_vhi = sem("s_vt"), sem("s_vhi")
        s_swap, s_rmul, s_rot, s_rhi = sem("s_swap"), sem("s_rmul"), sem("s_rot"), sem("s_rhi")
        s_misc = sem("s_misc")
        s_z, s_abs, s_e, s_l, s_sp, s_sphi, s_splo = (sem("s_z"), sem("s_abs"), sem("s_e"), sem("s_l"), sem("s_sp"),
                                                      sem("s_sphi"), sem("s_splo"))
        s_u, s_zx, s_ysum, s_yshi, s_yslo = sem("s_u"), sem("s_zx"), sem("s_ysum"), sem("s_yshi"), sem("s_yslo")
        s_ahi, s_alo = sem("s_ahi"), sem("s_alo")
        s_zr, s_zd, s_yr = sem("s_zr"), sem("s_zd"), sem("s_yr")
        s_yraw, s_ysq, s_ystat, s_yrs = sem("s_yraw"), sem("s_ysq"), sem("s_ystat"), sem("s_yrs")
        s_yqhi, s_yqlo = sem("s_yqhi"), sem("s_yqlo")
        s_silu, s_yn, s_yf, s_yrhi, s_yrlo = sem("s_silu"), sem("s_yn"), sem("s_yf"), sem("s_yrhi"), sem("s_yrlo")
        s_gate, s_sig, s_madd, s_mhi, s_mlo = sem("s_gate"), sem("s_sig"), sem("s_madd"), sem("s_mhi"), sem("s_mlo")
        s_read = sem("s_read")
        s_xt, s_rsq, s_rehi, s_relo, s_acc = sem("s_xt"), sem("s_rsq"), sem("s_rehi"), sem("s_relo"), sem("s_acc")
        s_rst, s_rln, s_rrs = sem("s_rst"), sem("s_rln"), sem("s_rrs")
        s_halo, s_c0, s_c1, s_c2, s_gelu = sem("s_halo"), sem("s_c0"), sem("s_c1"), sem("s_c2"), sem("s_gelu")
        s_g, s_ghi, s_glo = sem("s_g"), sem("s_ghi"), sem("s_glo")
        s_cw, s_p, s_phi, s_plo = sem("s_cw"), sem("s_p"), sem("s_phi"), sem("s_plo")
        s_pg, s_y, s_out = sem("s_pg"), sem("s_y"), sem("s_out")

        def width(i):
            return SEQ - P * i

        def read(tile):
            return tile - (OUT0 - 17)

        def a_sq(j, t):
            return A_T + t if isinstance(j, int) else A_SQ

        def sb_unit(n):
            return n // NT, NT - 1 - n % NT

        def r_unit(n):
            return n // NT, n % NT

        def sp_cols(hd, i):
            at = 1280 if (hd == 1 and i == 3) else (0, 512, 896, 1152)[i]
            return at, at + width(i)

        def sp_view(t, hd, i):
            a, b = sp_cols(hd, i)
            return t[:, T_SP:T_SP + 3, :].rearrange("p t n -> p (t n)")[:, a:b]

        block = ctx.enter_context(nc.Block())

        @block.sync
        def _(sp):
            def load(c, r, src, kt, first=False):
                if not first:
                    sp.wait_ge(s_wlo, c - 2)
                sp.dma_start(w_f[r][:, 0:kt, :], src).then_inc(s_wdma[r], 16)

            def load_x(i):
                sp.dma_start(fs[:, A_X + 2 * i:A_X + 2 * i + 2, :], xT[:, 2 * i:2 * i + 2, :]).then_inc(s_x[i], 16)

            load(0, 0, w_in[0], 8, first=True)
            for i in range(4):
                load_x(i)
            load(1, 1, w_in[1], 8, first=True)
            sp.dma_start(cst[:, :, :], consts).then_inc(s_cst, 16)
            load(2, 2, w_in[2], 8, first=True)
            sp.dma_start(fs[:, A_COS:A_COS + 2, :], rope[:, :, :]).then_inc(s_rope, 16)
            for c in range(3, 8):
                load(c, c % RING, w_in[c], 8)

            def swap_halves(j, t):
                sp.wait_ge(s_evac, SLOTS * j + 4 + t)
                if t == 1:
                    sp.wait_ge(s_rot, 2 * j + 1)
                raw = A_RAW + (3 + t) % 2
                for b in range(4):
                    sp.dma_start(fs[32 * b:32 * b + 32, A_SWAP, :],
                                 fs[32 * (b ^ 1):32 * (b ^ 1) + 32, raw, :]).then_inc(s_swap, 16)

            def pair_loads(j, s):
                c = SLOTS * j + s + 5
                load(c, (s + 5) % RING, w_in[c], 8)
                if s == 4:
                    sp.wait_ge(s_h, 5)
                    swap_halves(j, 0)
                if s == 5:
                    swap_halves(j, 1)
                if s == 6:
                    sp.wait_ge(s_evac, SLOTS * j + 6)
                    sp.dma_start(fs[:, A_DEC:A_DEC + 2, :], decay[j]).then_inc(s_dec, 16)

            with sp.Fori(0, PAIRS - 1) as j:
                for s in range(3, 3 + SLOTS):
                    pair_loads(j, s)
            for s in range(3, 7):
                pair_loads(PAIRS - 1, s)
            load(GATE0 + 3, 0, w_in[GATE0 + 3], 8)
            load(GATE0 + 4, 1, w_a[0], 4)
            load(GATE0 + 5, 2, w_b[0], 8)
            with sp.Fori(0, 2) as it:
                for mm in range(3):
                    c = MERGE0 + 12 * it + 4 * mm
                    m = 3 * it + (mm + 1)
                    load(c, (4 * mm) % RING, w_in[GATE0 + 2 + 2 * m], 8)
                    load(c + 1, (4 * mm + 1) % RING, w_in[GATE0 + 3 + 2 * m], 8)
                    load(c + 2, (4 * mm + 2) % RING, w_a[m], 4)
                    load(c + 3, (4 * mm + 3) % RING, w_b[m], 8)
            load(OUT0 - 2, 0, w_a[7], 4)
            load(OUT0 - 1, 1, w_b[7], 8)
            load(OUT0, OUT0 % RING, w_out[0], 8)
            with sp.Fori(0, 2) as it:
                for mm in range(3):
                    m = 3 * it + (mm + 1)
                    load(OUT0 + m, (OUT0 + 1 + mm) % RING, w_out[m], 8)
            load(OUT0 + 7, (OUT0 + 7) % RING, w_out[7], 8)
            load(UP0, UP0 % RING, w_up[0], 8)
            load(UP0 + 1, (UP0 + 1) % RING, w_up[1], 8)
            with sp.Fori(0, 7) as it:
                for q in range(6):
                    u = 6 * it + (2 + q)
                    load(UP0 + u, (UP0 + 2 + q) % RING, w_up[u], 8)
            with sp.Fori(0, KD) as m:
                for t in range(3):
                    k0 = sum(DOWN_K[:t])
                    load(DOWN0 + 3 * m + t, t, w_down[m, :, k0:k0 + DOWN_K[t], :], DOWN_K[t])

            def load_ple(m):
                load(PLE0 + 2 * m, (2 * m) % RING, w_pg[m], 8)
                load(PLE0 + 2 * m + 1, (2 * m + 1) % RING, w_pp[m], PB)

            def store(m):
                sp.wait_ge(s_y, m + 1)
                sp.dma_start(outT[m], fs[:, A_X + m, :]).then_inc(s_out, 16)

            for m in range(KD):
                load_ple(m)
                if m >= 4:
                    store(m - 4)
            for m in range(4, KD):
                store(m)
            sp.wait_ge(s_out, 16 * KD)

        @block.gpsimd
        def _(pool):
            for col, src, n in ((G_SBQ, g_sbq, 4), (G_SBK, g_sbk, 4), (G_RET, g_ret, 8), (G_FFN, g_ffn, 8),
                                (G_PLE, g_ple, 8)):
                pool.dma_start(gain[:, col:col + n, 0], src).then_inc(s_gain, 16)
            pool.dma_start(cw[:, 0:3, :, 0], conv_w).then_inc(s_cw, 16)
            pool.dma_start(cw[:, 3, :, 0], conv_b).then_inc(s_cw, 16)

        @block.tensor
        def _(pe):
            mm = nc.tensor.matmul

            def split3(out, w1, w0, x1, x0, start, stop, skip=False):
                mm(out, w1, x1, start=start, stop=False, skip_group_check=skip)
                mm(out, w1, x0, start=False, stop=False, skip_group_check=skip)
                return mm(out, w0, x1, start=False, stop=stop, skip_group_check=skip)

            def chunk(c, r, b, kt, tile0, hooks=None, k_first=0, last=True, before=None):
                pe.wait_ge(s_wlo, c + 1)
                for k in range(kt):
                    if before and k in before:
                        pe.wait_ge(*before[k])
                    ins = split3(bank[b][:, :], w_hi[r][:, k, :], w_lo[r][:, k, :], hi[:, tile0 + k, :],
                                 lo[:, tile0 + k, :], start=(k_first + k == 0), stop=(last and k == kt - 1))
                    if k == kt - 1:
                        ins.then_inc(s_used, 1)
                    if hooks and k in hooks:
                        hooks[k]()

            def stat(w, src, done):
                return mm(misc[:, :], cst[:, w, :], fs[:, src, :], start=True, stop=True).then_inc(done, 1)

            def stat_qk(j, t, free):
                pe.wait_ge(s_sq, 2 * j + t + 1)
                if free is not None:
                    pe.wait_ge(*free)
                stat(C_BLOCK, a_sq(j, t), s_stat)

            def stat_y(j, hd, free):
                pe.wait_ge(s_yqlo, 2 * j + hd + 1)
                pe.wait_ge(*free)
                mm(misc[:, :], cr[:, C_ONES, :], hi[:, T_YQ[hd], :], start=True, stop=False)
                mm(misc[:, :], cr[:, C_ONES, :], lo[:, T_YQ[hd], :], start=False, stop=True).then_inc(s_ystat, 1)

            def turn_v(j, s, free):
                pe.wait_ge(s_evac, SLOTS * j + s + 1)
                pe.wait_ge(*free)
                for i in range(NT):
                    ins = nc.tensor.transpose(misc[:, i * P:(i + 1) * P],
                                              fs[:, A_RAW + RAW_OF[s] % 2, i * P:(i + 1) * P],
                                              cst[:, C_IDENT, :])
                ins.then_inc(s_vt, 1)

            def sb_step(j, n):
                if n < 8:
                    hd, i = sb_unit(n)
                    N = width(i)
                    if n == 0:
                        pe.wait_ge(s_raw_done, RAWS * j + 2)
                    if n >= 3:
                        pe.wait_ge(s_zx, 8 * j + n - 2)
                    rows = slice(64 * hd, 64 * hd + 64)
                    z = zbank[n % 3][:, 0:N]
                    keys, qs = slice(i * P, (i + 1) * P), slice(i * P, SEQ)
                    split3(z, hi[rows, T_SBK, keys], lo[rows, T_SBK, keys], hi[rows, T_SBQ, qs], lo[rows, T_SBQ, qs],
                           start=True, stop=False, skip=True)
                    mm(zbank[n % 3][:, 0:P], cr[:, C_IDENT, :], cr[:, C_MASK, :], start=False, stop=True,
                       skip_group_check=True).then_inc(s_z, 1)
                if n >= 2:
                    u = n - 2
                    hd, i = sb_unit(u)
                    N = width(i)
                    pe.wait_ge(s_splo, 8 * j + u + 1)
                    for ii in range(i, NT):
                        w = cr[:, C_NEGU if ii == i else C_NEG1, :]
                        for part in (hi, lo):
                            ins = mm(zbank[u % 3][:, (ii - i) * P:N], w, sp_view(part, hd, ii), start=False,
                                     stop=(ii == NT - 1 and part is lo), skip_group_check=True)
                    ins.then_inc(s_u, 1)

            def sb_values(j, v):
                _, i = sb_unit(v)
                if v == 0:
                    pe.wait_ge(s_raw_done, RAWS * j + 3)
                if v == 4:
                    pe.wait_ge(s_yslo, 2 * j + 1)
                pe.wait_ge(s_alo, 16 * j + v + 1)
                cols = slice(i * P, (i + 1) * P)
                ins = split3(ybank[:, i * P:SEQ], hi[:, T_SBV, cols], lo[:, T_SBV, cols],
                             hi[:, T_A + v % 2, 0:width(i)], lo[:, T_A + v % 2, 0:width(i)],
                             start=(v % NT == 0), stop=(v % NT == 3), skip=True)
                if v % NT == 3:
                    ins.then_inc(s_ysum, 1)

            def r_step(j, n):
                if n < 8:
                    hd, i = r_unit(n)
                    if n == 0:
                        pe.wait_ge(s_raw_done, RAWS * j + 5)
                    if n >= 3:
                        pe.wait_ge(s_zd, 8 * j + n - 2)
                    rows = slice(64 * hd, 64 * hd + 64)
                    keys, qs = slice(i * P, (i + 1) * P), slice(i * P, SEQ)
                    split3(zbank[n % 3][:, 0:width(i)], hi[rows, T_RK, keys], lo[rows, T_RK, keys], hi[rows, T_RQ, qs],
                           lo[rows, T_RQ, qs], start=True, stop=True).then_inc(s_zr, 1)
                if n >= 1:
                    v = n - 1
                    hd, i = r_unit(v)
                    if v == 0:
                        pe.wait_ge(s_yslo, 2 * j + 2)
                        pe.wait_ge(s_raw_done, RAWS * j + 6)
                    if v == 4:
                        pe.wait_ge(s_raw_done, RAWS * j + 7)
                        pe.wait_ge(s_yraw, 2 * j + 1)
                    pe.wait_ge(s_alo, 16 * j + 8 + v + 1)
                    cols = slice(i * P, (i + 1) * P)
                    ins = split3(ybank[:, i * P:SEQ], hi[:, T_RV + hd, cols], lo[:, T_RV + hd, cols],
                                 hi[:, T_A + v % 2, 0:width(i)], lo[:, T_A + v % 2, 0:width(i)],
                                 start=(i == 0), stop=(i == 3), skip=True)
                    if i == 3:
                        ins.then_inc(s_yr, 1)

            def free_bank(j, s):
                pe.wait_ge(s_evac, SLOTS * j + s - 2)

            def front(j, prev):
                for s in range(3):
                    free_bank(j, s)
                    hooks = {1: lambda: r_step(prev, 3 * s), 4: lambda: r_step(prev, 3 * s + 1),
                             7: lambda: r_step(prev, 3 * s + 2)}
                    if s == 0:
                        hooks[6] = lambda: turn_v(prev, 8, (s_raw_done, RAWS * j - 1))
                    if s == 1:
                        hooks[5] = lambda: stat_qk(j, 0, (s_raw_done, RAWS * j))
                    if s == 2:
                        hooks[3] = lambda: stat_qk(j, 1, (s_misc, 4 * j - 1))
                        hooks[6] = lambda: stat_y(prev, 0, (s_misc, 4 * j))
                    chunk(SLOTS * j + s, s % RING, s % 3, KD, T_H, hooks)

            def back(j, prev):
                late = 1 if prev is None else 0
                places = {}
                for n in range(10):
                    slot, k = 3 + (n + late) // 2, (3, 7)[(n + late) % 2]
                    places[slot, k] = lambda n=n: sb_step(j, n)
                    if n >= 3:
                        slot, k = (slot, 5) if k == 3 else (slot + 1, 1)
                        places[slot, k] = lambda n=n: sb_values(j, n - 3)
                places[8, 7] = lambda: sb_values(j, 7)
                places[8, 6] = lambda: turn_v(j, 7, (s_raw_done, RAWS * j + 5))
                if prev is None:
                    places[3, 1] = lambda: stat_qk(0, 1, (s_misc, 1))
                    places[4, 2] = lambda: turn_v(0, 2, (s_misc, 2))
                else:
                    places[3, 4] = lambda: turn_v(j, 2, (s_misc, 4 * j + 1))
                    places[4, 2] = lambda: stat_y(prev, 1, (s_raw_done, RAWS * j + 3))
                for s in range(3, SLOTS):
                    free_bank(j, s)
                    hooks = {k: places[s, k] for k in range(KD) if (s, k) in places}
                    raw = prev is None and s < RAW_X
                    before = {k: (s_h, 1 + max(H_ORDER.index(x) for x in range(k + 1)))
                              for k in range(KD)} if prev is None and s == RAW_X else None
                    chunk(SLOTS * j + s, s % RING, s % 3, KD, T_X0 if raw else T_H, hooks, before=before)

            def stat_x():
                pe.wait_ge(s_cst, 16)
                pe.wait_ge(s_xacc, KD)
                stat(C_ONES, A_G, s_xst)

            chunk(0, 0, 0, KD, T_X0, before={k: (s_xlo, k + 1) for k in range(KD)})
            chunk(1, 1, 1, KD, T_X0, {6: stat_x})
            chunk(2, 2, 2, KD, T_X0, {7: lambda: stat_qk(0, 0, (s_xrs, 1))})
            back(0, None)
            with pe.Fori(1, PAIRS) as j:
                front(j, j - 1)
                back(j, j - 1)

            last = PAIRS - 1
            for s in range(3):
                free_bank(PAIRS, s)
                hooks = {1: lambda: r_step(last, 3 * s), 4: lambda: r_step(last, 3 * s + 1),
                         7: lambda: r_step(last, 3 * s + 2)}
                if s == 0:
                    hooks[5] = lambda: turn_v(last, 8, (s_raw_done, RAWS * PAIRS - 1))
                if s == 2:
                    hooks[3] = lambda: stat_y(last, 0, (s_raw_done, RAWS * PAIRS))
                chunk(GATE0 + s, s, s, KD, T_H, hooks)
            pe.wait_ge(s_gate, 1)
            chunk(GATE0 + 3, 0, 0, KD, T_H, {3: lambda: stat_y(last, 1, (s_misc, 4 * PAIRS - 1))})

            def branch_a(c, r, m):
                chunk(c, r, r, 4, T_YS)

            def branch_b(c, r, m, before=None):
                chunk(c, r, r, KD, T_YR, before=before)

            pe.wait_ge(s_gate, 2)
            branch_a(GATE0 + 4, 1, 0)
            pe.wait_ge(s_gate, 3)
            branch_b(GATE0 + 5, 2, 0, before={6: (s_yrlo, 7), 7: (s_yrlo, 8)})
            with pe.Fori(0, 2) as it:
                for q in range(3):
                    c = MERGE0 + 12 * it + 4 * q
                    m = 3 * it + (q + 1)
                    pe.wait_ge(s_gate, 2 * m + 2)
                    chunk(c, (4 * q) % 3, (4 * q) % 3, KD, T_H)
                    pe.wait_ge(s_read, 2 * m - 1)
                    chunk(c + 1, (4 * q + 1) % 3, (4 * q + 1) % 3, KD, T_H)
                    pe.wait_ge(s_read, 2 * m)
                    branch_a(c + 2, (4 * q + 2) % 3, m)
                    pe.wait_ge(s_gate, 2 * m + 3)
                    branch_b(c + 3, (4 * q + 3) % 3, m)
            pe.wait_ge(s_gate, 16)
            branch_a(OUT0 - 2, 0, 7)
            pe.wait_ge(s_read, 13)
            branch_b(OUT0 - 1, 1, 7)

            def tile(t, b, c, r, kt, tile0, **kw):
                pe.wait_ge(s_read, read(t) - 3)
                chunk(c, r, b, kt, tile0, **kw)

            def out_tile(m, b, **kw):
                tile(OUT0 + m, b, OUT0 + m, b, KD, T_M, **kw)

            out_tile(0, OUT0 % 3, before={k: (s_mlo, k + 1) for k in range(KD)})
            with pe.Fori(0, 2) as it:
                for q in range(3):
                    out_tile(3 * it + (q + 1), (OUT0 + q + 1) % 3)
            out_tile(7, (OUT0 + 7) % 3)

            def stat_res(n):
                pe.wait_ge(s_acc, KD * n)
                stat(C_ONES, A_ACC, s_rst)

            def up(u, b, **kw):
                tile(UP0 + u, b, UP0 + u, b, KD, T_H, **kw)

            up(0, UP0 % 3, hooks={7: lambda: stat_res(1)}, before={k: (s_relo, k + 1) for k in range(KD)})
            up(1, (UP0 + 1) % 3)
            with pe.Fori(0, 7) as it:
                for q in range(6):
                    up(6 * it + (q + 2), (UP0 + 2 + q) % 3)

            def down(m, b, before=None):
                pe.wait_ge(s_read, read(DOWN0 + m) - 3)
                for t in range(3):
                    k0 = sum(DOWN_K[:t])
                    chunk(DOWN0 + 3 * m + t, t, b, DOWN_K[t], T_G + k0, k_first=k0, last=(t == 2),
                          before=before if t == 2 else None)

            down(0, 0, before={DOWN_K[2] - 2: (s_glo, FB - 1), DOWN_K[2] - 1: (s_glo, FB)})
            with pe.Fori(0, 2) as it:
                for q in range(3):
                    down(3 * it + (q + 1), (q + 1) % 3)
            down(7, 7 % 3)

            def ple(m, q, **kw):
                t = PLET0 + 2 * m
                c = PLE0 + 2 * m
                tile(t, (PLET0 + 2 * q) % 3, c, (2 * q) % 3, KD, T_H, **kw)
                tile(t + 1, (PLET0 + 2 * q + 1) % 3, c + 1, (2 * q + 1) % 3, PB, T_P)

            pe.wait_ge(s_plo, 1)
            ple(0, 0, hooks={7: lambda: stat_res(2)}, before={k: (s_relo, KD + k + 1) for k in range(KD)})
            with pe.Fori(0, 2) as it:
                for q in range(3):
                    ple(3 * it + (q + 1), q + 1)
            ple(7, 7)

        @block.scalar
        def _(act):
            def run(out, src, func, done, **kw):
                return nc.scalar.activation(out, src, func, **kw).then_inc(done, 1)

            def ln_exp_tables():
                nc.scalar.preload_act_table_set("natural_log_exp_and_others")

            act.dma_start(gain[:, G_MIX:G_MIX + KD, 0], g_mix).then_inc(s_gmix, 16)
            act.wait_ge(s_eps, 1)
            ln_exp_tables()

            def high(third, r, kt=8, first=False):
                act.wait_ge(s_wdma[r], 16 * (third + 1))
                if not first:
                    act.wait_ge(s_used, 3 * third + r - 2)
                nc.scalar.copy(w_hi[r][:, 0:kt, :], w_f[r][:, 0:kt, :]).then_inc(s_whi, 1)

            def raw_square(k):
                if k >= 4:
                    act.wait_ge(s_xacc, k - 3)
                run(fs[:, A_T + k % 4, :], fs[:, A_X + k, :], ACT.Square, s_xsq)

            act.wait_ge(s_gmix, 16)
            for k in range(KD):
                if k == 0:
                    high(0, 0, first=True)
                if k % 2 == 0:
                    act.wait_ge(s_x[k // 2], 16)
                run(hi[:, T_X0 + k, :], fs[:, A_X + k, :], ACT.Identity, s_xhi, scale=gain[:, G_MIX + k, :])
                if k in (3, 5):
                    raw_square(k // 2 - 1)
            high(0, 1, first=True)
            for k in range(2, KD):
                raw_square(k)

            def evac(j, s):
                act.wait_ge(s_used, SLOTS * j + s + 1)
                if s in RAW_OF:
                    n = RAW_OF[s]
                    act.wait_ge(s_raw_done, RAWS * j + n - (1 if n else 0))
                    dst = fs[:, A_RAW + n % 2, :]
                else:
                    if s == 5:
                        act.wait_ge(s_yf, 2 * j)
                    dst = fs[:, A_G + s - 5, :]
                nc.scalar.copy(dst, bank[s % 3][:, :]).then_inc(s_evac, 1)

            def norm_qk(j, t, free):
                act.wait_ge(s_stat, 2 * j + t + 1)
                sq = fs[:, a_sq(j, t), :]
                run(sq, misc[:, :], ACT.Ln, s_misc, scale=1.0 / 64, bias=eps[:, :])
                act.wait_ge(s_misc, free)
                run(sq, sq, ACT.Exp, s_rs, scale=-0.5)

            def norm_y(j, hd, free):
                act.wait_ge(s_ystat, 2 * j + hd + 1)
                run(fs[:, A_SQY[hd], :], misc[:, :], ACT.Ln, s_misc, scale=1.0 / P, bias=eps[:, :])
                act.wait_ge(s_misc, free)
                run(fs[:, A_SQY[hd], :], fs[:, A_SQY[hd], :], ACT.Exp, s_yrs, scale=-0.5)

            def high_qk(j, t):
                act.wait_ge(s_nrm, 2 * j + t + 1)
                nc.scalar.copy(hi[:, T_SBQ + t, :], fs[:, A_RAW + t, :]).then_inc(s_nhi, 1)

            def high_rot(j, t):
                act.wait_ge(s_rot, 2 * j + t + 1)
                nc.scalar.copy(hi[:, T_RQ + t, :], fs[:, A_RAW + (3 + t) % 2, :]).then_inc(s_rhi, 1)

            def high_v(j, n):
                act.wait_ge(s_vt, 3 * j + n + 1)
                nc.scalar.copy(hi[:, (T_SBV, T_RV, T_RV + 1)[n], :], misc[:, :]).then_inc(s_vhi, 1)

            def high_y(j, hd):
                act.wait_ge(s_yf, 2 * j + hd + 1)
                nc.scalar.copy(hi[:, T_YR + hd + 2 * j, :], fs[:, A_Y + hd, :]).then_inc(s_yrhi, 1)

            def r_high(j, n):
                _, i = r_unit(n)
                act.wait_ge(s_zd, 8 * j + n + 1)
                nc.scalar.copy(hi[:, T_A + n % 2, 0:width(i)], fs[:, A_A + n % 2, 0:width(i)]).then_inc(s_ahi, 1)

            def y_raw(j, hd):
                act.wait_ge(s_yr, 2 * j + hd + 1)
                nc.scalar.copy(fs[:, A_Y + hd, :], ybank[:, :]).then_inc(s_yraw, 1)

            def y_square(j, hd):
                act.wait_ge(s_yraw, 2 * j + hd + 1)
                run(fs[:, A_SQY[hd], :], fs[:, A_Y + hd, :], ACT.Square, s_ysq)
                act.wait_ge(s_ysq, 2 * j + hd + 1)
                nc.scalar.copy(hi[:, T_YQ[hd], :], fs[:, A_SQY[hd], :]).then_inc(s_yqhi, 1)

            def silu(j):
                act.wait_ge(s_evac, SLOTS * j + 7)
                g = fs[:, A_G:A_G + 2, :]
                run(g, g, ACT.Silu, s_silu)
                ln_exp_tables()

            def y_high(j, hd):
                rows = slice(64 * hd, 64 * hd + 64)
                act.wait_ge(s_ysum, 2 * j + hd + 1)
                nc.scalar.copy(hi[rows, T_YS + j, :], ybank[rows, :]).then_inc(s_yshi, 1)

            def sb_step(j, n, beside=None):
                u = n - 2
                if 2 <= n < 10:
                    N = width(sb_unit(u)[1])
                    act.wait_ge(s_u, 8 * j + u + 1)
                    run(fs[:, A_A + u % 2, 0:N], zbank[u % 3][:, 0:N], ACT.Exp, s_zx)
                if beside:
                    beside()
                if n < 8:
                    _, i = sb_unit(n)
                    t = fs[:, A_T + n % 2, 0:width(i)]
                    act.wait_ge(s_abs, 8 * j + n + 1)
                    run(t, t, ACT.Exp, s_e, scale=-1.0)
                    act.wait_ge(s_e, 8 * j + n + 1)
                    run(t, t, ACT.Ln, s_l, bias=1.0)
                if 2 <= n < 10:
                    act.wait_ge(s_zx, 8 * j + u + 1)
                    nc.scalar.copy(hi[:, T_A + u % 2, 0:N], fs[:, A_A + u % 2, 0:N]).then_inc(s_ahi, 1)
                if n < 8:
                    hd, i = sb_unit(n)
                    act.wait_ge(s_sp, 8 * j + n + 1)
                    if n >= 5:
                        act.wait_ge(s_u, 8 * j + 4)
                    nc.scalar.copy(sp_view(hi, hd, i), fs[:, A_T + n % 2, 0:width(i)]).then_inc(s_sphi, 1)

            def ahead(j, s):
                q = s + 2
                high(3 * j + q // 3, q % 3)

            def start():
                high(0, 2, first=True)
                act.wait_ge(s_xst, 1)
                run(fs[:, A_RS, :], misc[:, :], ACT.Ln, s_xln, scale=1.0 / D, bias=eps[:, :])
                act.wait_ge(s_xln, 1)
                run(fs[:, A_RS, :], fs[:, A_RS, :], ACT.Exp, s_xrs, scale=-0.5)
                high_h(0)
                ahead(0, 1)
                high_h(1)
                norm_qk(0, 0, 1)
                ahead(0, 2)
                high_qk(0, 0)
                norm_qk(0, 1, 2)
                high_qk(0, 1)
                high_h(2)
                high_h(6)

            def high_h(k):
                act.wait_ge(s_hf, H_ORDER.index(k) + 1)
                nc.scalar.copy(hi[:, T_H + k, :], fs[:, A_X + k, :]).then_inc(s_hhi, 1)

            def front(j, prev):
                evac(prev, 8)
                r_high(prev, 0)
                ahead(j, 0)
                r_high(prev, 1)
                r_high(prev, 2)
                high_v(prev, 2)
                ahead(j, 1)
                evac(j, 0)
                r_high(prev, 3)
                y_raw(prev, 0)
                r_high(prev, 4)
                norm_qk(j, 0, 4 * j - 1)
                r_high(prev, 5)
                y_square(prev, 0)
                evac(j, 1)
                r_high(prev, 6)
                high_qk(j, 0)
                norm_qk(j, 1, 4 * j)
                r_high(prev, 7)
                high_qk(j, 1)
                ahead(j, 2)
                norm_y(prev, 0, 4 * j + 1)
                y_raw(prev, 1)
                y_square(prev, 1)

            def first_back():
                sb_early(0, 0)
                act.wait_ge(s_h, H_ORDER.index(6) + 1)
                nc.scalar.copy(fs[:, A_RS2, :], fs[:, A_RS, :]).then_inc(s_xrs, 1)
                sb_late(0, 0)
                ahead(0, 3)
                high_v(0, 0)
                sb_early(0, 1)
                sb_late(0, 1)
                high_h(4)
                ahead(0, 4)
                sb_step(0, 2)
                sb_step(0, 3)
                high_rot(0, 0)
                ahead(0, 5)
                sb_step(0, 4)
                high_h(3)
                sb_step(0, 5)
                high_h(5)
                ahead(0, 6)
                sb_step(0, 6, lambda: y_high(0, 0))
                sb_step(0, 7)
                high_rot(0, 1)
                ahead(0, 7)
                high_h(7)
                sb_step(0, 8)
                ahead(0, 8)
                sb_step(0, 9)
                silu(0)
                high_v(0, 1)
                y_high(0, 1)

            def back(j, prev):
                evac(j, 2)
                ahead(j, 3)
                sb_early(j, 0)
                high_v(j, 0)
                sb_late(j, 0)
                sb_early(j, 1)
                high_y(prev, 0)
                sb_late(j, 1)
                ahead(j, 4)
                evac(j, 3)
                sb_step(j, 2)
                norm_y(prev, 1, 4 * j + 2)
                sb_step(j, 3)
                high_y(prev, 1)
                evac(j, 4)
                sb_step(j, 4)
                ahead(j, 5)
                sb_step(j, 5)
                high_rot(j, 0)
                ahead(j, 6)
                evac(j, 5)
                sb_step(j, 6, lambda: y_high(j, 0))
                sb_step(j, 7)
                high_rot(j, 1)
                evac(j, 6)
                ahead(j, 7)
                sb_step(j, 8)
                silu(j)
                sb_step(j, 9)
                evac(j, 7)
                ahead(j, 8)
                high_v(j, 1)
                y_high(j, 1)

            def sb_early(j, n):
                _, i = sb_unit(n)
                t = fs[:, A_T + n % 2, 0:width(i)]
                act.wait_ge(s_abs, 8 * j + n + 1)
                run(t, t, ACT.Exp, s_e, scale=-1.0)
                act.wait_ge(s_e, 8 * j + n + 1)
                run(t, t, ACT.Ln, s_l, bias=1.0)

            def sb_late(j, n):
                hd, i = sb_unit(n)
                act.wait_ge(s_sp, 8 * j + n + 1)
                nc.scalar.copy(sp_view(hi, hd, i), fs[:, A_T + n % 2, 0:width(i)]).then_inc(s_sphi, 1)

            start()
            first_back()
            with act.Fori(1, PAIRS) as j:
                front(j, j - 1)
                back(j, j - 1)

            last = PAIRS - 1

            def raw_gate(n):
                act.wait_ge(s_used, GATE0 + n + 1)
                nc.scalar.copy(fs[:, A_SG[n // 2] + n % 2, :], bank[n % 3][:, :]).then_inc(s_gate, 1)

            evac(last, 8)
            r_high(last, 0)
            ahead(PAIRS, 0)
            r_high(last, 1)
            high_v(last, 2)
            r_high(last, 2)
            ahead(PAIRS, 1)
            raw_gate(0)
            r_high(last, 3)
            y_raw(last, 0)
            r_high(last, 4)
            y_square(last, 0)
            r_high(last, 5)
            high((GATE0 + 4) // 3, 1, 4)
            raw_gate(1)
            r_high(last, 6)
            r_high(last, 7)
            norm_y(last, 0, 4 * PAIRS - 1)
            y_raw(last, 1)
            y_square(last, 1)
            high((GATE0 + 5) // 3, 2)
            high_y(last, 0)
            raw_gate(2)
            norm_y(last, 1, 4 * PAIRS)
            high_y(last, 1)
            high(MERGE0 // 3, 0)
            raw_gate(3)
            for m in range(2):
                act.wait_ge(s_gate, 2 * m + 2)
                g = fs[:, A_SG[m]:A_SG[m] + 2, :]
                run(g, g, ACT.Sigmoid, s_sig)
            high(MERGE0 // 3, 1)
            act.wait_ge(s_yrlo, 8)
            act.dma_start(fs[:, A_X:A_X + 8, :], xT).then_inc(s_xt, 16)

            def high_merged(m, ring):
                act.wait_ge(s_madd, m + 1)
                nc.scalar.copy(hi[:, T_M + m, :], fs[:, A_SG[ring], :]).then_inc(s_mhi, 1)

            def gate(c, q, t):
                act.wait_ge(s_used, c + t + 1)
                run(fs[:, A_SG[(q + 2) % 3] + t, :], bank[(4 * q + t) % 3][:, :], ACT.Sigmoid, s_gate)

            with act.Fori(0, 2) as it:
                for q in range(3):
                    c = MERGE0 + 12 * it + 4 * q
                    m = 3 * it + (q + 1)

                    def two_ahead(t, kt=8):
                        high(MERGE0 // 3 + 4 * it + (4 * q + t + 2) // 3, (4 * q + t + 2) % 3, kt)

                    two_ahead(0, 4)
                    high_merged(m - 1, q)
                    two_ahead(1)
                    gate(c, q, 0)
                    two_ahead(2)
                    gate(c, q, 1)
                    two_ahead(3)
            high(OUT0 // 3, OUT0 % 3)
            high_merged(6, 0)
            high((OUT0 + 1) // 3, (OUT0 + 1) % 3)
            high((OUT0 + 2) // 3, (OUT0 + 2) % 3)
            high_merged(7, 1)

            def residual(t, n, col):
                act.wait_ge(s_read, read(t))
                x = fs[:, A_X + n, :]
                run(fs[:, A_SQR, :], x, ACT.Square, s_rsq)
                run(hi[:, T_H + n, :], x, ACT.Identity, s_rehi, scale=gain[:, col + n, :])

            def norm_res(n):
                ln_exp_tables()
                act.wait_ge(s_rst, n)
                run(fs[:, A_RS, :], misc[:, :], ACT.Ln, s_rln, scale=1.0 / D, bias=eps[:, :])
                act.wait_ge(s_rln, n)
                run(fs[:, A_RS, :], fs[:, A_RS, :], ACT.Exp, s_rrs, scale=-0.5)

            high((OUT0 + 3) // 3, (OUT0 + 3) % 3)
            residual(OUT0, 0, G_FFN)
            with act.Fori(0, 2) as it:
                for q in range(3):
                    c = OUT0 + 4 + q
                    high(c // 3 + it, c % 3)
                    n = 3 * it + (q + 1)
                    residual(OUT0 + n, n, G_FFN)

            def conv_gelu(f):
                act.wait_ge(s_read, read(UP0 + 2 * f))
                run(fs[:, A_C, :], fs_flat[:, A_CONV * SEQ + 2:A_CONV * SEQ + 2 + SEQ], ACT.Identity, s_c0,
                    scale=cw[:, 2, f, :], bias=cw[:, 3, f, :])
                act.wait_ge(s_c2, f + 1)
                run(fs[:, A_C, :], fs[:, A_C, :], ACT.Gelu_apprx_tanh, s_gelu)

            def high_g(f):
                act.wait_ge(s_g, f + 1)
                nc.scalar.copy(hi[:, T_G + f, :], fs[:, A_U, :]).then_inc(s_ghi, 1)

            high((UP0 + 2) // 3, (UP0 + 2) % 3)
            residual(OUT0 + 7, 7, G_FFN)
            high((UP0 + 3) // 3, (UP0 + 3) % 3)
            norm_res(1)
            act.wait_ge(s_cw, 32)
            conv_gelu(0)
            act.wait_ge(s_mlo, KD)
            act.dma_start(fs[:, A_P:A_P + PB, :], pT).then_inc(s_p, 16)
            with act.Fori(0, 7) as it:
                for q in range(3):
                    c = UP0 + 4 + 2 * q
                    f = 3 * it + (q + 1)
                    high(c // 3 + 2 * it, c % 3)
                    high_g(f - 1)
                    high((c + 1) // 3 + 2 * it, (c + 1) % 3)
                    conv_gelu(f)

            def down_ahead(m, t):
                u = t + 2
                high(DOWN0 // 3 + m + u // 3, u % 3, DOWN_K[u % 3])

            down_ahead(0, 0)
            high_g(FB - 1)
            down_ahead(0, 1)
            act.wait_ge(s_p, 16)
            nc.scalar.copy(hi[:, T_P:T_P + PB, :], fs[:, A_P:A_P + PB, :]).then_inc(s_phi, 1)
            down_ahead(0, 2)
            down_ahead(1, 0)
            residual(DOWN0, 0, G_PLE)
            down_ahead(1, 1)
            down_ahead(1, 2)
            with act.Fori(0, 2) as it:
                for q in range(3):
                    n = 3 * it + (q + 1)
                    down_ahead(n + 1, 0)
                    residual(DOWN0 + n, n, G_PLE)
                    high(DOWN0 // 3 + n + 2, 0, 8)
                    high(DOWN0 // 3 + n + 2, 1, 8)

            def ple_ahead(c):
                if c < PLE0 + 2 * KD:
                    high(c // 3, c % 3, PB if c % 2 else 8)

            def ple_gate(m):
                act.wait_ge(s_read, read(PLET0 + 2 * m))
                run(fs[:, A_U, :], fs[:, A_U, :], ACT.Sigmoid, s_pg)

            ple_ahead(PLE0 + 2)
            residual(DOWN0 + 7, 7, G_PLE)
            ple_ahead(PLE0 + 3)
            norm_res(2)
            ple_gate(0)
            for m in range(1, KD):
                ple_ahead(PLE0 + 2 * m + 2)
                ple_ahead(PLE0 + 2 * m + 3)
                ple_gate(m)

        @block.vector
        def _(dve):
            def tt(out, a, b, op, done):
                return nc.vector.tensor_tensor(out, a, b, op).then_inc(done, 1)

            def stt(out, a, scalar, b, op0, op1, done):
                return nc.vector.scalar_tensor_tensor(out=out, in0=a, scalar=scalar, in1=b, op0=op0,
                                                      op1=op1).then_inc(done, 1)

            def low(third, r, kt=8):
                dve.wait_ge(s_whi, 3 * third + r + 1)
                tt(w_lo[r][:, 0:kt, :], w_f[r][:, 0:kt, :], w_hi[r][:, 0:kt, :], ALU.subtract, s_wlo)

            nc.vector.memset(eps[:, :], EPS).then_inc(s_eps, 1)
            def raw_split(k):
                dve.wait_ge(s_xhi, k + 1)
                stt(lo[:, T_X0 + k, :], fs[:, A_X + k, :], gain[:, G_MIX + k, :], hi[:, T_X0 + k, :], ALU.mult,
                    ALU.subtract, s_xlo)

            def raw_sum(k):
                acc, sq = fs[:, A_G, :], fs[:, A_T + k % 4, :]
                dve.wait_ge(s_xsq, k + 1)
                if k == 0:
                    nc.vector.tensor_copy(acc, sq).then_inc(s_xacc, 1)
                else:
                    dve.wait_ge(s_xacc, k)
                    tt(acc, acc, sq, ALU.add, s_xacc)

            low(0, 0)
            dve.wait_ge(s_gmix, 16)
            for k in range(KD):
                raw_split(k)
                if k in (3, 5):
                    raw_sum(k // 2 - 1)
            low(0, 1)
            for k in range(2, KD):
                raw_sum(k)
            low(0, 2)
            dve.wait_ge(s_cst, 16)
            nc.vector.tensor_copy(cr[:, :, :], cst[:, :, :]).then_inc(s_cr, 1)
            dve.wait_ge(s_gain, 16 * 5)
            g8 = gain[:, G_SBQ:G_SBQ + PAIRS, 0]
            nc.vector.tensor_scalar(g8, g8, 0.125, None, ALU.mult).then_inc(s_cr, 1)
            dve.wait_ge(s_cr, 2)

            def normed(k):
                x = fs[:, A_X + k, :]
                rs = A_RS if k in (0, 1, 2, 6) else A_RS2
                stt(x, x, gain[:, G_MIX + k, :], fs[:, rs, :], ALU.mult, ALU.mult, s_hf)

            def low_h(k):
                dve.wait_ge(s_hhi, H_ORDER.index(k) + 1)
                tt(lo[:, T_H + k, :], fs[:, A_X + k, :], hi[:, T_H + k, :], ALU.subtract, s_h)

            def evac_x(s):
                dve.wait_ge(s_used, s + 1)
                if s < 2:
                    dve.wait_ge(s_h, s + 1)
                elif s in RAW_OF:
                    dve.wait_ge(s_raw_done, RAW_OF[s] - 1)
                dst = A_RAW + RAW_OF[s] % 2 if s in RAW_OF else A_G + s - 5
                tt(fs[:, dst, :], bank[s % 3][:, :], fs[:, A_RS if s < 3 else A_RS2, :], ALU.mult, s_evac)

            def square(j, t):
                dve.wait_ge(s_evac, SLOTS * j + t + 1)
                r = fs[:, A_RAW + t, :]
                if t == 1 and not isinstance(j, int):
                    dve.wait_ge(s_nrm, 2 * j + 1)
                tt(fs[:, a_sq(j, t), :], r, r, ALU.mult, s_sq)

            def norm(j, t):
                dve.wait_ge(s_rs, 2 * j + t + 1)
                r = fs[:, A_RAW + t, :]
                col = (G_SBQ, G_SBK)[t]
                stt(r, r, gain[:, col + j, :], fs[:, a_sq(j, t), :], ALU.mult, ALU.mult, s_nrm)

            def low_qk(j, t):
                dve.wait_ge(s_nhi, 2 * j + t + 1)
                tt(lo[:, T_SBQ + t, :], fs[:, A_RAW + t, :], hi[:, T_SBQ + t, :], ALU.subtract, s_raw_done)

            def rotate(j, t):
                dve.wait_ge(s_swap, 64 * (2 * j + t + 1))
                raw, other = fs[:, A_RAW + (3 + t) % 2, :], fs[:, A_SWAP, :]
                tt(raw, raw, fs[:, A_COS, :], ALU.mult, s_rmul)
                tt(other, other, fs[:, A_COS + 1, :], ALU.mult, s_rmul)

            def rotate_sum(j, t):
                raw, other = fs[:, A_RAW + (3 + t) % 2, :], fs[:, A_SWAP, :]
                dve.wait_ge(s_rmul, 4 * j + 2 * t + 2)
                tt(raw, raw, other, ALU.add, s_rot)

            def low_rot(j, t):
                dve.wait_ge(s_rhi, 2 * j + t + 1)
                tt(lo[:, T_RQ + t, :], fs[:, A_RAW + (3 + t) % 2, :], hi[:, T_RQ + t, :], ALU.subtract, s_raw_done)

            def low_v(j, n):
                dve.wait_ge(s_vhi, 3 * j + n + 1)
                t = (T_SBV, T_RV, T_RV + 1)[n]
                nc.vector.tensor_tensor(lo[:, t, :], misc[:, :], hi[:, t, :], ALU.subtract).then_inc(s_raw_done, 1)

            def r_scores(j, n):
                hd, i = r_unit(n)
                N = width(i)
                if n == 0:
                    dve.wait_ge(s_dec, 16 * (j + 1))
                dve.wait_ge(s_zr, 8 * j + n + 1)
                tt(fs[:, A_A + n % 2, 0:N], zbank[n % 3][:, 0:N], fs[:, A_DEC + hd, 0:N], ALU.mult, s_zd)

            def r_low(j, n):
                _, i = r_unit(n)
                N = width(i)
                dve.wait_ge(s_ahi, 16 * j + 8 + n + 1)
                tt(lo[:, T_A + n % 2, 0:N], fs[:, A_A + n % 2, 0:N], hi[:, T_A + n % 2, 0:N], ALU.subtract, s_alo)

            def y_square_low(j, hd):
                dve.wait_ge(s_yqhi, 2 * j + hd + 1)
                t = T_YQ[hd]
                tt(lo[:, t, :], fs[:, A_SQY[hd], :], hi[:, t, :], ALU.subtract, s_yqlo)

            def y_norm(j, hd):
                dve.wait_ge(s_yrs, 2 * j + hd + 1)
                y = fs[:, A_Y + hd, :]
                col = G_RET + hd + 2 * j
                stt(y, y, gain[:, col, :], fs[:, A_SQY[hd], :], ALU.mult, ALU.mult, s_yn)

            def y_swish(j, hd):
                y = fs[:, A_Y + hd, :]
                dve.wait_ge(s_silu, j + 1)
                dve.wait_ge(s_yn, 2 * j + hd + 1)
                tt(y, y, fs[:, A_G + hd, :], ALU.mult, s_yf)

            def low_y(j, hd):
                dve.wait_ge(s_yrhi, 2 * j + hd + 1)
                t = T_YR + hd + 2 * j
                tt(lo[:, t, :], fs[:, A_Y + hd, :], hi[:, t, :], ALU.subtract, s_yrlo)

            def sb_abs(j, n):
                N = width(sb_unit(n)[1])
                dve.wait_ge(s_z, 8 * j + n + 1)
                nc.vector.tensor_scalar(fs[:, A_T + n % 2, 0:N].bitcast(I32), zbank[n % 3][:, 0:N].bitcast(I32),
                                        0x7FFFFFFF, None, ALU.bitwise_and).then_inc(s_abs, 1)

            def sb_softplus(j, n):
                N = width(sb_unit(n)[1])
                t = fs[:, A_T + n % 2, 0:N]
                dve.wait_ge(s_l, 8 * j + n + 1)
                stt(t, zbank[n % 3][:, 0:N], 0.0, t, ALU.max, ALU.add, s_sp)

            def sb_low(j, n):
                hd, i = sb_unit(n)
                dve.wait_ge(s_sphi, 8 * j + n + 1)
                tt(sp_view(lo, hd, i), fs[:, A_T + n % 2, 0:width(i)], sp_view(hi, hd, i), ALU.subtract, s_splo)

            def y_low(j, hd):
                rows = slice(64 * hd, 64 * hd + 64)
                dve.wait_ge(s_yshi, 2 * j + hd + 1)
                tt(lo[rows, T_YS + j, :], ybank[rows, :], hi[rows, T_YS + j, :], ALU.subtract, s_yslo)

            def sb_step(j, n, beside=None, after=None):
                if n < 8:
                    sb_abs(j, n)
                    if beside:
                        beside()
                    sb_softplus(j, n)
                if 2 <= n < 10:
                    u = n - 2
                    N = width(sb_unit(u)[1])
                    dve.wait_ge(s_ahi, 16 * j + u + 1)
                    tt(lo[:, T_A + u % 2, 0:N], fs[:, A_A + u % 2, 0:N], hi[:, T_A + u % 2, 0:N], ALU.subtract,
                       s_alo)
                if after:
                    after()
                if n < 8:
                    sb_low(j, n)

            def ahead(j, s):
                q = s + 2
                low(3 * j + q // 3, q % 3)

            def start():
                dve.wait_ge(s_xrs, 1)
                normed(0)
                normed(1)
                low_h(0)
                evac_x(0)
                square(0, 0)
                ahead(0, 1)
                low_h(1)
                evac_x(1)
                square(0, 1)
                normed(2)
                norm(0, 0)
                ahead(0, 2)
                low_qk(0, 0)
                norm(0, 1)
                low_qk(0, 1)
                low_h(2)
                normed(6)
                evac_x(2)
                dve.wait_ge(s_rope, 16)

            def first_back():
                sb_abs(0, 0)
                low_h(6)
                sb_softplus(0, 0)
                dve.wait_ge(s_xrs, 2)
                evac_x(3)
                sb_low(0, 0)
                ahead(0, 3)
                low_v(0, 0)
                sb_abs(0, 1)
                normed(4)
                sb_softplus(0, 1)
                sb_low(0, 1)
                low_h(4)
                ahead(0, 4)
                sb_step(0, 2)
                evac_x(4)
                sb_step(0, 3, lambda: rotate(0, 0), lambda: rotate_sum(0, 0))
                low_rot(0, 0)
                ahead(0, 5)
                sb_step(0, 4, lambda: normed(3))
                evac_x(5)
                sb_step(0, 5, lambda: normed(5))
                low_h(3)
                ahead(0, 6)
                sb_step(0, 6, lambda: y_low(0, 0), lambda: low_h(5))
                sb_step(0, 7, lambda: rotate(0, 1), lambda: rotate_sum(0, 1))
                low_rot(0, 1)
                normed(7)
                evac_x(6)
                ahead(0, 7)
                sb_step(0, 8)
                low_h(7)
                evac_x(7)
                ahead(0, 8)
                sb_step(0, 9)
                low_v(0, 1)
                y_low(0, 1)

            def front(j, prev):
                r_scores(prev, 0)
                r_low(prev, 0)
                ahead(j, 0)
                r_scores(prev, 1)
                r_low(prev, 1)
                r_scores(prev, 2)
                r_low(prev, 2)
                low_v(prev, 2)
                ahead(j, 1)
                r_scores(prev, 3)
                square(j, 0)
                r_low(prev, 3)
                r_scores(prev, 4)
                r_low(prev, 4)
                r_scores(prev, 5)
                norm(j, 0)
                r_low(prev, 5)
                r_scores(prev, 6)
                square(j, 1)
                r_low(prev, 6)
                low_qk(j, 0)
                y_square_low(prev, 0)
                r_scores(prev, 7)
                norm(j, 1)
                r_low(prev, 7)
                low_qk(j, 1)
                ahead(j, 2)

            def back(j, prev):
                ahead(j, 3)
                sb_abs(j, 0)
                y_square_low(prev, 1)
                y_norm(prev, 0)
                sb_softplus(j, 0)
                low_v(j, 0)
                sb_low(j, 0)
                sb_abs(j, 1)
                y_swish(prev, 0)
                sb_softplus(j, 1)
                sb_low(j, 1)
                low_y(prev, 0)
                ahead(j, 4)
                sb_step(j, 2)
                sb_step(j, 3, lambda: y_norm(prev, 1), lambda: y_swish(prev, 1))
                low_y(prev, 1)
                sb_step(j, 4, lambda: rotate(j, 0), lambda: rotate_sum(j, 0))
                ahead(j, 5)
                sb_step(j, 5)
                low_rot(j, 0)
                ahead(j, 6)
                sb_step(j, 6, lambda: y_low(j, 0))
                sb_step(j, 7, lambda: rotate(j, 1), lambda: rotate_sum(j, 1))
                low_rot(j, 1)
                ahead(j, 7)
                sb_step(j, 8)
                sb_step(j, 9)
                ahead(j, 8)
                low_v(j, 1)
                y_low(j, 1)

            start()
            first_back()
            with dve.Fori(1, PAIRS) as j:
                front(j, j - 1)
                back(j, j - 1)

            last = PAIRS - 1
            r_scores(last, 0)
            r_low(last, 0)
            ahead(PAIRS, 0)
            r_scores(last, 1)
            r_low(last, 1)
            low_v(last, 2)
            r_scores(last, 2)
            r_low(last, 2)
            ahead(PAIRS, 1)
            for n in range(3, 6):
                r_scores(last, n)
                r_low(last, n)
            y_square_low(last, 0)
            low((GATE0 + 4) // 3, 1, 4)
            for n in range(6, 8):
                r_scores(last, n)
                r_low(last, n)
            y_norm(last, 0)
            y_swish(last, 0)
            y_square_low(last, 1)
            low((GATE0 + 5) // 3, 2)
            low_y(last, 0)
            y_norm(last, 1)
            y_swish(last, 1)
            low_y(last, 1)

            def branch(m, t, used, b, ring):
                g = fs[:, A_SG[ring] + t, :]
                dve.wait_ge(s_used, used)
                tt(g, bank[b][:, :], g, ALU.mult, s_read)

            def merge(m, ring):
                g0, g1 = fs[:, A_SG[ring], :], fs[:, A_SG[ring] + 1, :]
                dve.wait_ge(s_read, 2 * m + 2)
                tt(g0, g0, g1, ALU.add, s_madd)

            def low_merged(m, ring):
                dve.wait_ge(s_mhi, m + 1)
                tt(lo[:, T_M + m, :], fs[:, A_SG[ring], :], hi[:, T_M + m, :], ALU.subtract, s_mlo)

            low(MERGE0 // 3, 0)
            low(MERGE0 // 3, 1)
            dve.wait_ge(s_sig, 1)
            branch(0, 0, GATE0 + 5, 1, 0)
            with dve.Fori(0, 2) as it:
                for q in range(3):
                    c = MERGE0 + 12 * it + 4 * q
                    m = 3 * it + (q + 1)

                    def two_ahead(t, kt=8):
                        low(MERGE0 // 3 + 4 * it + (4 * q + t + 2) // 3, (4 * q + t + 2) % 3, kt)

                    two_ahead(0, 4)
                    branch(m - 1, 1, c, (4 * q + 2) % 3, q)
                    merge(m - 1, q)
                    two_ahead(1)
                    low_merged(m - 1, q)
                    two_ahead(2)
                    two_ahead(3)
                    dve.wait_ge(s_gate, 2 * m + 2)
                    branch(m, 0, c + 3, (4 * q + 2) % 3, (q + 1) % 3)
            low(OUT0 // 3, OUT0 % 3)
            branch(6, 1, OUT0 - 2, 2, 0)
            merge(6, 0)
            low((OUT0 + 1) // 3, (OUT0 + 1) % 3)
            low_merged(6, 0)
            dve.wait_ge(s_gate, 16)
            branch(7, 0, OUT0 - 1, 0, 1)
            low((OUT0 + 2) // 3, (OUT0 + 2) % 3)
            branch(7, 1, OUT0, 1, 1)
            merge(7, 1)
            low_merged(7, 1)

            def residual(n, phase, col, used, b):
                x = fs[:, A_X + n, :]
                dve.wait_ge(s_used, used)
                tt(x, x, bank[b][:, :], ALU.add, s_read)
                at = KD * phase + n + 1
                dve.wait_ge(s_rehi, at)
                stt(lo[:, T_H + n, :], x, gain[:, col + n, :], hi[:, T_H + n, :], ALU.mult, ALU.subtract,
                    s_relo)
                dve.wait_ge(s_rsq, at)
                acc, sq = fs[:, A_ACC, :], fs[:, A_SQR, :]
                if isinstance(n, int) and n == 0:
                    nc.vector.tensor_copy(acc, sq).then_inc(s_acc, 1)
                else:
                    dve.wait_ge(s_acc, at - 1)
                    tt(acc, acc, sq, ALU.add, s_acc)

            low((OUT0 + 3) // 3, (OUT0 + 3) % 3)
            dve.wait_ge(s_xt, 16)
            residual(0, 0, G_FFN, OUT0 + 1, OUT0 % 3)
            with dve.Fori(0, 2) as it:
                for q in range(3):
                    c = OUT0 + 4 + q
                    low(c // 3 + it, c % 3)
                    n = 3 * it + (q + 1)
                    residual(n, 0, G_FFN, OUT0 + n + 1, (OUT0 + q + 1) % 3)

            a_pad = fs_flat[:, A_CONV * SEQ:A_CONV * SEQ + SEQ + 2]
            cv, rs = fs[:, A_C, :], fs[:, A_RS, :]

            def gate_path(f, b):
                dve.wait_ge(s_used, UP0 + 2 * f + 1)
                tt(a_pad[:, 2:], bank[b][:, :], rs, ALU.mult, s_read)
                dve.wait_ge(s_c0, f + 1)
                stt(cv, a_pad[:, 1:SEQ + 1], cw[:, 1, f, :], cv, ALU.mult, ALU.add, s_c1)
                dve.wait_ge(s_c1, f + 1)
                stt(cv, a_pad[:, 0:SEQ], cw[:, 0, f, :], cv, ALU.mult, ALU.add, s_c2)

            def value_path(f, b):
                u = fs[:, A_U, :]
                dve.wait_ge(s_used, UP0 + 2 * f + 2)
                tt(u, bank[b][:, :], rs, ALU.mult, s_read)
                dve.wait_ge(s_gelu, f + 1)
                dve.wait_ge(s_read, read(UP0 + 1 + 2 * f))
                tt(u, u, cv, ALU.mult, s_g)
                dve.wait_ge(s_ghi, f + 1)
                tt(lo[:, T_G + f, :], u, hi[:, T_G + f, :], ALU.subtract, s_glo)

            low((UP0 + 2) // 3, (UP0 + 2) % 3)
            residual(7, 0, G_FFN, OUT0 + 8, (OUT0 + 7) % 3)
            nc.vector.memset(a_pad[:, 0:2], 0.0).then_inc(s_halo, 1)
            dve.wait_ge(s_halo, 1)
            low((UP0 + 3) // 3, (UP0 + 3) % 3)
            dve.wait_ge(s_rrs, 1)
            gate_path(0, UP0 % 3)
            with dve.Fori(0, 7) as it:
                for q in range(3):
                    c = UP0 + 4 + 2 * q
                    f = 3 * it + (q + 1)
                    low(c // 3 + 2 * it, c % 3)
                    value_path(f - 1, (UP0 + 1 + 2 * q) % 3)
                    low((c + 1) // 3 + 2 * it, (c + 1) % 3)
                    gate_path(f, (UP0 + 2 + 2 * q) % 3)

            def down_ahead(m, t):
                u = t + 2
                low(DOWN0 // 3 + m + u // 3, u % 3, DOWN_K[u % 3])

            down_ahead(0, 0)
            value_path(FB - 1, (DOWN0 - 1) % 3)
            down_ahead(0, 1)
            dve.wait_ge(s_phi, 1)
            tt(lo[:, T_P:T_P + PB, :], fs[:, A_P:A_P + PB, :], hi[:, T_P:T_P + PB, :], ALU.subtract, s_plo)
            down_ahead(0, 2)
            down_ahead(1, 0)
            residual(0, 1, G_PLE, DOWN0 + 3, DOWN0 % 3)
            down_ahead(1, 1)
            down_ahead(1, 2)
            with dve.Fori(0, 2) as it:
                for q in range(3):
                    n = 3 * it + (q + 1)
                    down_ahead(n + 1, 0)
                    residual(n, 1, G_PLE, DOWN0 + 3 * n + 3, (DOWN0 + q + 1) % 3)
                    low(DOWN0 // 3 + n + 2, 0, 8)
                    low(DOWN0 // 3 + n + 2, 1, 8)

            def ple_ahead(c):
                if c < PLE0 + 2 * KD:
                    low(c // 3, c % 3, PB if c % 2 else 8)

            t = fs[:, A_U, :]

            def ple_gate(m):
                dve.wait_ge(s_used, PLE0 + 2 * m + 1)
                if m >= 1:
                    dve.wait_ge(s_y, m)
                tt(t, bank[(PLET0 + 2 * m) % 3][:, :], rs, ALU.mult, s_read)

            def ple_out(m):
                x = fs[:, A_X + m, :]
                dve.wait_ge(s_pg, m + 1)
                dve.wait_ge(s_used, PLE0 + 2 * m + 2)
                tt(t, bank[(PLET0 + 2 * m + 1) % 3][:, :], t, ALU.mult, s_read)
                dve.wait_ge(s_read, read(PLET0 + 2 * m + 1))
                tt(x, x, t, ALU.add, s_y)

            ple_ahead(PLE0 + 2)
            residual(7, 1, G_PLE, PLE0, (DOWN0 + 7) % 3)
            ple_ahead(PLE0 + 3)
            dve.wait_ge(s_rrs, 2)
            ple_gate(0)
            for m in range(1, KD):
                ple_ahead(PLE0 + 2 * m + 2)
                ple_out(m - 1)
                ple_ahead(PLE0 + 2 * m + 3)
                ple_gate(m)
            ple_out(KD - 1)


def _chunks(w):
    k, n = w.shape
    return w.reshape(k // P, P, n // P, P).transpose(2, 1, 0, 3)


def _constants(np):
    i = np.arange(P)
    consts = np.zeros((P, N_CONST, P), np.float32)
    consts[:, C_ONES] = 1.0
    consts[:, C_BLOCK] = (i[:, None] // 64 == i[None, :] // 64)
    consts[:, C_IDENT] = np.eye(P)
    consts[:, C_NEGU] = -1.0 * (i[:, None] >= i[None, :])
    consts[:, C_NEG1] = -1.0
    consts[:, C_MASK] = np.where(i[:, None] >= i[None, :], -1e30, 0.0)
    heads = np.arange(2 * PAIRS)
    log_gamma = np.log1p(-np.exp2(-5.0 - heads))
    diff = np.arange(SEQ)[None, :] - i[:, None]
    decay = np.where(diff >= 0, np.exp(np.maximum(diff, 0)[None] * log_gamma[:, None, None]), 0.0) * 64 ** -0.5
    decay = decay.reshape(PAIRS, 2, P, SEQ).transpose(0, 2, 1, 3).astype(np.float32)
    half = i % 32
    inv = (np.float32(10000.0) ** (-half.astype(np.float32) * np.float32(2.0) / np.float32(64))).astype(np.float32)
    ang = (np.arange(SEQ, dtype=np.float32)[None, :] * inv[:, None]).astype(np.float64)
    sign = np.where(i % 64 < 32, -1.0, 1.0)[:, None]
    rope = np.stack([np.cos(ang), sign * np.sin(ang)], axis=1).astype(np.float32)
    return consts, decay, rope


def kernel(**inputs):
    import numpy as np
    import concourse.bacc as bacc
    from concourse.bass_utils import run_bass_kernel_spmd as run

    a = {name: np.asarray(value) for name, value in inputs.items()}
    blocks = _chunks(a["w_in"][0])
    order = []
    for j in range(PAIRS):
        order += [j, 4 + j, 8 + j, 12 + j, 16 + j, 28 + 2 * j, 29 + 2 * j, 20 + 2 * j, 21 + 2 * j]
    for m in range(KD):
        order += [36 + m, 44 + m]
    ups = _chunks(a["w_up"][0])
    up_order = [x for f in range(FB) for x in (f, FB + f)]
    consts, decay, rope = _constants(np)

    def cols(v, n):
        return v.reshape(n, P).T

    laid = {
        "xT": a["x"][0].T.reshape(KD, P, SEQ).transpose(1, 0, 2),
        "pT": a["p"][0, 0].T.reshape(PB, P, SEQ).transpose(1, 0, 2),
        "w_in": blocks[order], "w_a": _chunks(a["w_branch_sb"][0]), "w_b": _chunks(a["w_branch_ret"][0]),
        "w_out": _chunks(a["w_out"][0]), "w_up": ups[up_order], "w_down": _chunks(a["w_down"][0]),
        "w_pg": _chunks(a["w_ple_gate"][0]), "w_pp": _chunks(a["w_ple_proj"][0]),
        "g_mix": cols(a["g_mix"], KD), "g_ffn": cols(a["g_ffn"], KD), "g_ple": cols(a["g_ple"], KD),
        "g_ret": cols(a["ret_norm_gain"], 8), "g_sbq": cols(a["sb_q_gain"], PAIRS),
        "g_sbk": cols(a["sb_k_gain"], PAIRS),
        "conv_w": a["conv_w"][0].reshape(3, FB, P).transpose(2, 0, 1), "conv_b": cols(a["conv_b"], FB),
        "consts": consts, "decay": decay, "rope": rope,
    }
    nc = bacc.Bacc("TRN2", target_bir_lowering=False, num_devices=1)
    arrays, args = {}, []
    for name, value in laid.items():
        value = np.ascontiguousarray(value)
        arrays[f"in_{name}"] = value
        args.append(nc.dram_tensor(f"in_{name}", value.shape, mybir.dt.from_np(value.dtype), kind="ExternalInput").ap())
    args.append(nc.dram_tensor("out_t", (KD, P, SEQ), F32, kind="ExternalOutput").ap())
    build(nc, *args)
    got = run(nc, [arrays], core_ids=[0]).results[0]["out_t"]
    return np.ascontiguousarray(np.asarray(got).reshape(D, SEQ).T[None])
```
